# Optimizing a Trainium2 kernel written in Bass

```python
import jax, jax.numpy as jnp
from jax import lax
import numpy as np

D_MODEL = 2048
BATCH = 1
SEQ = 256
DEPTH = 1

MIX_WIDTH = D_MODEL
FOURIER_WIDTH = MIX_WIDTH // 2
N_FOURIER_GROUPS = 4
FOURIER_GROUP_DIM = FOURIER_WIDTH // N_FOURIER_GROUPS
ATTN_WIDTH = MIX_WIDTH - FOURIER_WIDTH
HEAD_DIM = 128
N_HEADS = ATTN_WIDTH // HEAD_DIM
WINDOW_DILATIONS = ((128, 1), (512, 4), (2048, 16))
D_FF = 4 * D_MODEL
IN_WIDTH = FOURIER_WIDTH + 3 * ATTN_WIDTH
RMS_EPS = 1e-6


def _rmsnorm(x, g):
    xf = x.astype(jnp.float32)
    inv = lax.rsqrt(jnp.mean(xf * xf, axis=-1, keepdims=True) + RMS_EPS)
    return (xf * inv * g.astype(jnp.float32)).astype(x.dtype)

def _alibi_slopes(n_heads):
    return jnp.asarray(2.0 ** (-8.0 * (np.arange(n_heads) + 1) / n_heads), dtype=jnp.float32)

def _dilated_branch(q, k, v, slopes, dilation, radius):
    B, H, S, Dh = q.shape
    M = S // dilation
    blk = radius
    nb = -(-M // blk)
    Mp = nb * blk

    def to_classes(t):
        return t.reshape(B, H, M, dilation, Dh).transpose(0, 1, 3, 2, 4)

    pad0 = ((0, 0), (0, 0), (0, 0))
    qc = jnp.pad(to_classes(q), pad0 + ((0, Mp - M), (0, 0))).reshape(B, H, dilation, nb, blk, Dh)
    kc = jnp.pad(to_classes(k), pad0 + ((blk, Mp - M + blk), (0, 0))).reshape(B, H, dilation, nb + 2, blk, Dh)
    vc = jnp.pad(to_classes(v), pad0 + ((blk, Mp - M + blk), (0, 0))).reshape(B, H, dilation, nb + 2, blk, Dh)
    kw = jnp.concatenate([kc[:, :, :, :-2], kc[:, :, :, 1:-1], kc[:, :, :, 2:]], axis=4)
    vw = jnp.concatenate([vc[:, :, :, :-2], vc[:, :, :, 1:-1], vc[:, :, :, 2:]], axis=4)

    mq = jnp.arange(nb)[:, None, None] * blk + jnp.arange(blk)[None, :, None]
    mk = jnp.arange(nb)[:, None, None] * blk - blk + jnp.arange(3 * blk)[None, None, :]
    rel = mk - mq
    valid = (jnp.abs(rel) <= radius) & (mk >= 0) & (mk < M)
    dist = (dilation * jnp.abs(rel)).astype(jnp.float32)

    s = jnp.einsum('bhrnqd,bhrnkd->bhrnqk', qc, kw).astype(jnp.float32)
    s = s - slopes[None, :, None, None, None, None] * dist
    s = jnp.where(valid, s, -jnp.inf)
    mx = jnp.max(s, axis=-1, keepdims=True)
    p = jnp.exp(s - mx)
    den = jnp.sum(p, axis=-1)
    o = jnp.einsum('bhrnqk,bhrnkd->bhrnqd', p.astype(v.dtype), vw).astype(jnp.float32) / den[..., None]

    def from_classes(t):
        tail = t.shape[5:]
        t = t.reshape((B, H, dilation, Mp) + tail)[:, :, :, :M]
        t = jnp.moveaxis(t, 2, 3)
        return t.reshape((B, H, S) + tail)

    return from_classes(o), from_classes(mx[..., 0]), from_classes(den)

def _dilated_attention(q, k, v):
    slopes = _alibi_slopes(q.shape[1])
    outs, maxes, dens = [], [], []
    for window, dil in WINDOW_DILATIONS:
        o, m, d = _dilated_branch(q, k, v, slopes, dil, (window // 2) // dil)
        outs.append(o); maxes.append(m); dens.append(d)
    mx = jnp.stack(maxes)
    w = jnp.stack(dens) * jnp.exp(mx - jnp.max(mx, axis=0, keepdims=True))
    o = jnp.sum(w[..., None] * jnp.stack(outs), axis=0) / jnp.sum(w, axis=0)[..., None]
    return o

def _fourier_mix(u, w_f):
    B, S, _ = u.shape
    ug = u.reshape(B, S, N_FOURIER_GROUPS, FOURIER_GROUP_DIM).astype(jnp.float32)
    re = jnp.fft.fft2(ug, axes=(1, 3), norm="ortho").real.astype(u.dtype)
    y = jnp.einsum('bsgc,gce->bsge', re, w_f)
    return y.reshape(B, S, FOURIER_WIDTH)

def first_inputs(seed: int = 0) -> dict:
    key = jax.random.key(seed)
    ks = jax.random.split(key, 10)
    f32 = jnp.float32
    x = jax.random.normal(ks[0], (BATCH, SEQ, D_MODEL), f32)
    norm_mix_g = 1.0 + 0.02 * jax.random.normal(ks[1], (DEPTH, D_MODEL), f32)
    w_in = jax.random.normal(ks[2], (DEPTH, D_MODEL, IN_WIDTH), f32) * D_MODEL ** -0.5
    w_fourier = jax.random.normal(ks[3], (DEPTH, N_FOURIER_GROUPS, FOURIER_GROUP_DIM, FOURIER_GROUP_DIM), f32) * FOURIER_GROUP_DIM ** -0.5
    w_out = jax.random.normal(ks[4], (DEPTH, MIX_WIDTH, D_MODEL), f32) * MIX_WIDTH ** -0.5
    norm_mlp_g = 1.0 + 0.02 * jax.random.normal(ks[5], (DEPTH, D_MODEL), f32)
    w_up = jax.random.normal(ks[6], (DEPTH, D_MODEL, D_FF), f32) * D_MODEL ** -0.5
    w_down = jax.random.normal(ks[7], (DEPTH, D_FF, D_MODEL), f32) * D_FF ** -0.5
    norm_final_g = 1.0 + 0.02 * jax.random.normal(ks[8], (D_MODEL,), f32)
    return {"x": x, "norm_mix_g": norm_mix_g, "w_in": w_in, "w_fourier": w_fourier,
            "w_out": w_out, "norm_mlp_g": norm_mlp_g, "w_up": w_up, "w_down": w_down,
            "norm_final_g": norm_final_g}

def first_block(x, norm_mix_g, w_in, w_fourier, w_out, norm_mlp_g, w_up, w_down, norm_final_g):
    B, S, _ = x.shape
    h = x
    for layer in range(DEPTH):
        u = _rmsnorm(h, norm_mix_g[layer])
        proj = jnp.einsum('bsd,de->bse', u, w_in[layer])
        u_f = proj[..., :FOURIER_WIDTH]
        qkv = proj[..., FOURIER_WIDTH:].reshape(B, S, 3, N_HEADS, HEAD_DIM)
        q = jnp.transpose(qkv[:, :, 0], (0, 2, 1, 3)) * (HEAD_DIM ** -0.5)
        k = jnp.transpose(qkv[:, :, 1], (0, 2, 1, 3))
        v = jnp.transpose(qkv[:, :, 2], (0, 2, 1, 3))
        y_f = _fourier_mix(u_f, w_fourier[layer])
        y_a = _dilated_attention(q, k, v).astype(h.dtype)
        y_a = jnp.transpose(y_a, (0, 2, 1, 3)).reshape(B, S, ATTN_WIDTH)
        y = jnp.concatenate([y_f, y_a], axis=-1)
        h = h + jnp.einsum('bse,ed->bsd', y, w_out[layer])
        u = _rmsnorm(h, norm_mlp_g[layer])
        a = jnp.einsum('bsd,df->bsf', u, w_up[layer])
        a = jnp.square(jax.nn.relu(a))
        h = h + jnp.einsum('bsf,fd->bsd', a, w_down[layer])
    return _rmsnorm(h, norm_final_g)


CTX_LEN = 256
GRID_W = 64
N_DIR = 2
MIX_WIDTH_2 = D_MODEL
GLA_HEADS = 4
GLA_WIDTH = MIX_WIDTH_2 // 2
GLA_DV = GLA_WIDTH // GLA_HEADS
GLA_DK = GLA_DV // 2
GLA_LR = 16
GLA_NORMALIZER = 16.0
MLSTM_HEADS = 4
MLSTM_WIDTH = MIX_WIDTH_2 - GLA_WIDTH
MLSTM_DV = MLSTM_WIDTH // MLSTM_HEADS
MLSTM_DK = MLSTM_DV // 2
CHUNK = 64
D_FF_2 = 128 * ((8 * D_MODEL // 3 + 127) // 128)
CONV_K = 3
EPS = 1e-6

PROJ_SIZES = (GLA_HEADS * GLA_DK, GLA_HEADS * GLA_DK, GLA_WIDTH, GLA_WIDTH, GLA_LR,
              MLSTM_HEADS * MLSTM_DK, MLSTM_HEADS * MLSTM_DK, MLSTM_WIDTH, MLSTM_WIDTH,
              N_DIR * 2 * MLSTM_HEADS)
PROJ_WIDTH = sum(PROJ_SIZES)
PROJ_SPLITS = tuple(int(s) for s in np.cumsum(PROJ_SIZES)[:-1])


def rmsnorm(x, g):
    xf = x.astype(jnp.float32)
    y = xf * lax.rsqrt(jnp.mean(jnp.square(xf), axis=-1, keepdims=True) + EPS)
    return (y * g.astype(jnp.float32)).astype(x.dtype)

def _rev(t, d):
    return jnp.flip(t, axis=1) if d == 1 else t

def _chunk(t):
    b, t_len = t.shape[:2]
    t = t.reshape((b, t_len // CHUNK, CHUNK) + t.shape[2:])
    return jnp.swapaxes(jnp.moveaxis(t, 1, 0), 2, 3)

def _unchunk(t):
    n, b, h, c, d = t.shape
    return jnp.moveaxis(jnp.swapaxes(t, 2, 3), 0, 1).reshape(b, n * c, h, d)

def gla_scan(k, v, log_a, s0, q=None):
    tril = jnp.tril(jnp.ones((CHUNK, CHUNK), dtype=bool))
    xs = (_chunk(k), _chunk(v), _chunk(log_a)) + ((_chunk(q),) if q is not None else ())

    def step(s, inp):
        kc, vc, ac = inp[:3]
        bcum = jnp.cumsum(ac, axis=2)
        b_end = bcum[:, :, -1, :]
        k_to_end = kc * jnp.exp(b_end[:, :, None, :] - bcum)
        s_new = jnp.exp(b_end)[..., None] * s + jnp.einsum('bhik,bhiv->bhkv', k_to_end, vc)
        if q is None:
            return s_new, None
        qc = inp[3]
        rel = jnp.where(tril[:, :, None], bcum[:, :, :, None, :] - bcum[:, :, None, :, :], -jnp.inf)
        scores = jnp.einsum('bhjk,bhik,bhjik->bhji', qc, kc, jnp.exp(rel))
        o = (jnp.einsum('bhji,bhiv->bhjv', scores, vc)
             + jnp.einsum('bhjk,bhkv->bhjv', qc * jnp.exp(bcum), s))
        return s_new, o

    s_fin, o = lax.scan(step, s0, xs)
    return s_fin, (None if q is None else _unchunk(o))

def mlstm_scan(k, v, log_i, log_f, state0, q=None):
    tril = jnp.tril(jnp.ones((CHUNK, CHUNK), dtype=bool))
    xs = (_chunk(k), _chunk(v), _chunk(log_i), _chunk(log_f)) + ((_chunk(q),) if q is not None else ())

    def step(carry, inp):
        c, n, m = carry
        kc, vc, ic, fc = inp[:4]
        fcum = jnp.cumsum(fc, axis=-1)
        f_end = fcum[..., -1]
        w_log = f_end[..., None] - fcum + ic
        m_new = jnp.maximum(f_end + m, jnp.max(w_log, axis=-1))
        carry_scale = jnp.exp(f_end + m - m_new)
        w = jnp.exp(w_log - m_new[..., None])
        c_new = carry_scale[..., None, None] * c + jnp.einsum('bhi,bhik,bhiv->bhkv', w, kc, vc)
        n_new = carry_scale[..., None] * n + jnp.einsum('bhi,bhik->bhk', w, kc)
        if q is None:
            return (c_new, n_new, m_new), None
        qc = inp[4]
        d_log = jnp.where(tril, fcum[..., :, None] - fcum[..., None, :] + ic[..., None, :], -jnp.inf)
        inter_log = fcum + m[..., None]
        m_q = jnp.maximum(inter_log, jnp.max(d_log, axis=-1))
        s = jnp.einsum('bhjk,bhik->bhji', qc, kc) * jnp.exp(d_log - m_q[..., None])
        inter = jnp.exp(inter_log - m_q)
        num = (jnp.einsum('bhji,bhiv->bhjv', s, vc)
               + inter[..., None] * jnp.einsum('bhjk,bhkv->bhjv', qc, c))
        den = jnp.sum(s, axis=-1) + inter * jnp.einsum('bhjk,bhk->bhj', qc, n)
        h = num / jnp.maximum(jnp.abs(den), jnp.exp(-m_q))[..., None]
        return (c_new, n_new, m_new), h

    st_fin, h = lax.scan(step, state0, xs)
    return st_fin, (None if q is None else _unchunk(h))

def project_heads(h, w_in, gla_w_lr, gla_b_lr, mlstm_b_gate):
    b, t, _ = h.shape
    f32 = jnp.float32
    z = jnp.einsum('btd,dp->btp', h, w_in)
    gq, gk, gv, gg, glr, mq, mk, mv, mo, mgate = jnp.split(z, PROJ_SPLITS, axis=-1)
    gla_q = gq.reshape(b, t, GLA_HEADS, GLA_DK).astype(f32) * (GLA_DK ** -0.5)
    gla_k = gk.reshape(b, t, GLA_HEADS, GLA_DK).astype(f32)
    gla_v = gv.reshape(b, t, GLA_HEADS, GLA_DV).astype(f32)
    gla_gate = gg.reshape(b, t, GLA_HEADS, GLA_DV)
    dec = jnp.einsum('btr,zrk->zbtk', glr, gla_w_lr) + gla_b_lr[:, None, None, :]
    gla_loga = (jax.nn.log_sigmoid(dec.astype(f32)) / GLA_NORMALIZER).reshape(N_DIR, b, t, GLA_HEADS, GLA_DK)
    ml_q = mq.reshape(b, t, MLSTM_HEADS, MLSTM_DK).astype(f32)
    ml_k = mk.reshape(b, t, MLSTM_HEADS, MLSTM_DK).astype(f32) * (MLSTM_DK ** -0.5)
    ml_v = mv.reshape(b, t, MLSTM_HEADS, MLSTM_DV).astype(f32)
    ml_ogate = mo.reshape(b, t, MLSTM_HEADS, MLSTM_DV)
    pre = (mgate.reshape(b, t, N_DIR, 2, MLSTM_HEADS) + mlstm_b_gate).astype(f32)
    ml_logi = jnp.moveaxis(pre[:, :, :, 0], 2, 0)
    ml_logf = jnp.moveaxis(jax.nn.log_sigmoid(pre[:, :, :, 1]), 2, 0)
    scan_in = (gla_q, gla_k, gla_v, gla_loga, ml_q, ml_k, ml_v, ml_logi, ml_logf)
    return scan_in, (gla_gate, ml_ogate)

def recurrent_groups(lat, ctx, with_ctx_out):
    gq, gk, gv, ga, mq, mk, mv, mi, mf = lat
    cq, ck, cv, ca, cmq, cmk, cmv, cmi, cmf = ctx
    b = gq.shape[0]
    f32 = jnp.float32
    gla_lat, ml_lat, gla_ctx, ml_ctx = [], [], [], []
    for d in range(N_DIR):
        s0 = jnp.zeros((b, GLA_HEADS, GLA_DK, GLA_DV), f32)
        s_ctx, o_ctx = gla_scan(_rev(ck, d), _rev(cv, d), _rev(ca[d], d), s0,
                                _rev(cq, d) if with_ctx_out else None)
        _, o_lat = gla_scan(_rev(gk, d), _rev(gv, d), _rev(ga[d], d), s_ctx, _rev(gq, d))
        gla_lat.append(_rev(o_lat, d))
        st0 = (jnp.zeros((b, MLSTM_HEADS, MLSTM_DK, MLSTM_DV), f32),
               jnp.zeros((b, MLSTM_HEADS, MLSTM_DK), f32),
               jnp.zeros((b, MLSTM_HEADS), f32))
        st_ctx, h_ctx = mlstm_scan(_rev(cmk, d), _rev(cmv, d), _rev(cmi[d], d), _rev(cmf[d], d), st0,
                                   _rev(cmq, d) if with_ctx_out else None)
        _, h_lat = mlstm_scan(_rev(mk, d), _rev(mv, d), _rev(mi[d], d), _rev(mf[d], d), st_ctx, _rev(mq, d))
        ml_lat.append(_rev(h_lat, d))
        if with_ctx_out:
            gla_ctx.append(_rev(o_ctx, d))
            ml_ctx.append(_rev(h_ctx, d))
    lat_out = (gla_lat[0] + gla_lat[1], ml_lat[0] + ml_lat[1])
    ctx_out = (gla_ctx[0] + gla_ctx[1], ml_ctx[0] + ml_ctx[1]) if with_ctx_out else None
    return lat_out, ctx_out

def merge_groups(gla_o, ml_h, gla_gate, ml_ogate, gla_g_norm, mlstm_g_norm, w_out, dtype):
    b, t = gla_o.shape[:2]
    f32 = jnp.float32
    y_gla = rmsnorm(gla_o, gla_g_norm) * jax.nn.silu(gla_gate.astype(f32))
    y_ml = jax.nn.sigmoid(ml_ogate.astype(f32)) * rmsnorm(ml_h, mlstm_g_norm)
    y = jnp.concatenate([y_gla.reshape(b, t, GLA_WIDTH), y_ml.reshape(b, t, MLSTM_WIDTH)], axis=-1)
    return jnp.einsum('btm,md->btd', y.astype(dtype), w_out)

def conv_ffn(h, rows, cols, w_up, conv_w, conv_b, w_down):
    b, t, _ = h.shape
    u = jnp.einsum('btd,df->btf', h, w_up)
    u_gate, u_val = jnp.split(u, 2, axis=-1)
    g = lax.conv_general_dilated(u_gate.reshape(b, rows, cols, D_FF_2), conv_w[:, :, None, :],
                                 window_strides=(1, 1), padding='SAME',
                                 dimension_numbers=('NHWC', 'HWIO', 'NHWC'),
                                 feature_group_count=D_FF_2)
    g = g.reshape(b, t, D_FF_2) + conv_b
    return jnp.einsum('btf,fd->btd', jax.nn.silu(g) * u_val, w_down)

def trunk_layer(x, ctx, c_act, cc_act, w_mod, b_mod, g_norm1, g_norm2, w_in, gla_w_lr, gla_b_lr,
                mlstm_b_gate, gla_g_norm, mlstm_g_norm, w_out, w_up, conv_w, conv_b, w_down, update_ctx):
    b, t, _ = x.shape
    rows = t // GRID_W
    mod = (c_act @ w_mod + b_mod)[:, None, :]
    mod_c = (cc_act @ w_mod + b_mod)[None, None, :]
    sh1, sc1, gt1, sh2, sc2, gt2 = jnp.split(mod, 6, axis=-1)
    csh1, csc1, cgt1, csh2, csc2, cgt2 = jnp.split(mod_c, 6, axis=-1)

    h = rmsnorm(x, g_norm1) * (1 + sc1) + sh1
    hc = rmsnorm(ctx, g_norm1) * (1 + csc1) + csh1
    lat_in, lat_gates = project_heads(h, w_in, gla_w_lr, gla_b_lr, mlstm_b_gate)
    ctx_in, ctx_gates = project_heads(hc, w_in, gla_w_lr, gla_b_lr, mlstm_b_gate)
    (lat_gla, lat_ml), ctx_out = recurrent_groups(lat_in, ctx_in, update_ctx)
    x = x + gt1 * merge_groups(lat_gla, lat_ml, lat_gates[0], lat_gates[1],
                               gla_g_norm, mlstm_g_norm, w_out, x.dtype)

    h2 = rmsnorm(x, g_norm2) * (1 + sc2) + sh2
    x = x + gt2 * conv_ffn(h2, rows, GRID_W, w_up, conv_w, conv_b, w_down)

    if update_ctx:
        ctx = ctx + cgt1 * merge_groups(ctx_out[0], ctx_out[1], ctx_gates[0], ctx_gates[1],
                                        gla_g_norm, mlstm_g_norm, w_out, ctx.dtype)
        hc2 = rmsnorm(ctx, g_norm2) * (1 + csc2) + csh2
        ctx = ctx + cgt2 * conv_ffn(hc2, 1, ctx.shape[1], w_up, conv_w, conv_b, w_down)
    return x, ctx

def second_inputs(seed: int = 0) -> dict:
    key = jax.random.key(seed)
    ks = jax.random.split(key, 20)
    f32 = jnp.float32
    L = DEPTH

    def nrm(k, shape, s):
        return jax.random.normal(k, shape, f32) * s

    gate_base = jnp.array([0.0, 3.0], f32)[None, None, :, None]
    return {
        'x': nrm(ks[0], (BATCH, SEQ, D_MODEL), 1.0),
        'c': nrm(ks[1], (BATCH, D_MODEL), 1.0),
        'ctx': nrm(ks[2], (BATCH, CTX_LEN, D_MODEL), 1.0),
        'c_ctx': nrm(ks[3], (D_MODEL,), 1.0),
        'w_mod': nrm(ks[4], (L, D_MODEL, 6 * D_MODEL), D_MODEL ** -0.5),
        'b_mod': nrm(ks[5], (L, 6 * D_MODEL), 0.01),
        'g_norm1': 1.0 + nrm(ks[6], (L, D_MODEL), 0.05),
        'g_norm2': 1.0 + nrm(ks[7], (L, D_MODEL), 0.05),
        'w_in': nrm(ks[8], (L, D_MODEL, PROJ_WIDTH), D_MODEL ** -0.5),
        'gla_w_lr': nrm(ks[9], (L, N_DIR, GLA_LR, GLA_HEADS * GLA_DK), GLA_LR ** -0.5),
        'gla_b_lr': nrm(ks[10], (L, N_DIR, GLA_HEADS * GLA_DK), 0.1),
        'mlstm_b_gate': gate_base + nrm(ks[11], (L, N_DIR, 2, MLSTM_HEADS), 0.1),
        'gla_g_norm': 1.0 + nrm(ks[12], (L, GLA_DV), 0.05),
        'mlstm_g_norm': 1.0 + nrm(ks[13], (L, MLSTM_DV), 0.05),
        'w_out': nrm(ks[14], (L, MIX_WIDTH_2, D_MODEL), MIX_WIDTH_2 ** -0.5),
        'w_up': nrm(ks[15], (L, D_MODEL, 2 * D_FF_2), D_MODEL ** -0.5),
        'conv_w': nrm(ks[16], (L, CONV_K, CONV_K, D_FF_2), 1.0 / CONV_K),
        'conv_b': nrm(ks[17], (L, D_FF_2), 0.01),
        'w_down': nrm(ks[18], (L, D_FF_2, D_MODEL), D_FF_2 ** -0.5),
        'g_final': 1.0 + nrm(ks[19], (D_MODEL,), 0.05),
    }

def second_block(x, c, ctx, c_ctx, w_mod, b_mod, g_norm1, g_norm2, w_in, gla_w_lr, gla_b_lr, mlstm_b_gate,
              gla_g_norm, mlstm_g_norm, w_out, w_up, conv_w, conv_b, w_down, g_final):
    c_act = jax.nn.silu(c)
    cc_act = jax.nn.silu(c_ctx)
    for l in range(DEPTH):
        x, ctx = trunk_layer(x, ctx, c_act, cc_act, w_mod[l], b_mod[l], g_norm1[l], g_norm2[l], w_in[l],
                             gla_w_lr[l], gla_b_lr[l], mlstm_b_gate[l], gla_g_norm[l], mlstm_g_norm[l],
                             w_out[l], w_up[l], conv_w[l], conv_b[l], w_down[l],
                             update_ctx=(l < DEPTH - 1))
    return rmsnorm(x, g_final)


def setup_inputs(seed=0):
    out = dict(first_inputs(seed))
    for name, value in second_inputs(seed + 1).items():
        if name != "x":
            out[name + "_2"] = value
    return out


def reference(
    x, norm_mix_g, w_in, w_fourier, w_out, norm_mlp_g, w_up, w_down, norm_final_g, c_2, ctx_2,
    c_ctx_2, w_mod_2, b_mod_2, g_norm1_2, g_norm2_2, w_in_2, gla_w_lr_2, gla_b_lr_2,
    mlstm_b_gate_2, gla_g_norm_2, mlstm_g_norm_2, w_out_2, w_up_2, conv_w_2, conv_b_2, w_down_2,
    g_final_2,
):
    x = first_block(
        x, norm_mix_g, w_in, w_fourier, w_out, norm_mlp_g, w_up, w_down, norm_final_g,
    )
    return second_block(
        x, c_2, ctx_2, c_ctx_2, w_mod_2, b_mod_2, g_norm1_2, g_norm2_2, w_in_2, gla_w_lr_2,
        gla_b_lr_2, mlstm_b_gate_2, gla_g_norm_2, mlstm_g_norm_2, w_out_2, w_up_2, conv_w_2,
        conv_b_2, w_down_2, g_final_2,
    )


_drawn_inputs = setup_inputs


def setup_inputs(seed=0):
    import zlib

    import numpy as np

    out = dict(_drawn_inputs(seed))
    spreads = {}
    factors = {'norm_mix_g': 3.703,
     'b_mod_2': 2.698,
     'gla_g_norm_2': 3.257,
     'mlstm_g_norm_2': 4.619,
     'conv_b_2': 23.508,
     'norm_mlp_g': 3.173,
     'g_norm2_2': 3.252}
    for name, (base, spread) in spreads.items():
        noise = np.random.default_rng([zlib.crc32(name.encode()), seed]).standard_normal(out[name].shape)
        drawn = base * np.exp(spread * noise) if base else spread * noise
        out[name] = __import__('jax').numpy.asarray(drawn.astype(out[name].dtype))
    for name, factor in factors.items():
        out[name] = (out[name] * factor).astype(out[name].dtype)
    return out
```

```python
import numpy as np
import concourse.bass as bass
from concourse import mybir
from contextlib import ExitStack

F32 = mybir.dt.float32
F32R = mybir.dt.float32r
U8 = mybir.dt.uint8
ALU = mybir.AluOpType
ACT = mybir.ActivationFunctionType
AX = mybir.AxisListType

P = 128
TOK = 256
TC = TOK // P
D = 2048
KD = D // P
EPS = 1e-6
NG = 4
NH = 8
DH = 128
DFF1 = 4 * D
H = 4
DK = 128
DV = 256
LR = 16
DFF2 = 5504
F2 = DFF2 // P
NMODCH = 6 * KD
LEVELS = 7
NEG = -1.0e30

SLOTS = 8
TW = 1024
LEAD = 4
NBLK = 512
GROUPS1 = 4
GROUP2 = (16, 16, 11)

CONST_A = [("ident", P), ("flip", P), ("suf", P), ("pre", P), ("inc_f", P), ("inc_b", P), ("one16", P),
           ("ones", P), ("two_ident", P), ("sel4", 2)]
CONST_B = [("dft_pos", 2 * 512), ("dft_cos", 2 * 256), ("dft_nsin", 2 * 256), ("dist", 512), ("logcount", 512)]


def offsets(spec):
    out, at = {}, 0
    for name, n in spec:
        out[name] = (at, n)
        at += n
    return out, at


OFF_A, NA = offsets(CONST_A)
OFF_B, NB_ = offsets(CONST_B)

VEC = [("g_mix", KD), ("g_mlp", KD), ("g_n1", KD), ("g_n2", KD), ("c", KD), ("cc", KD), ("b_mod", NMODCH),
       ("conv_w", F2 * 9), ("conv_b", F2)]
OFF_V, NV = offsets(VEC)


class Phase:

    def __init__(self, name, kind, iters, blocks, main, mod=0, k=None, evac=None, dest=0, mod0=0):
        self.name, self.kind, self.iters, self.blocks = name, kind, iters, blocks
        self.main, self.mod, self.k, self.evac, self.dest, self.mod0 = main, mod, k, evac, dest, mod0
        self.per_block = main + mod
        self.per_iter = self.per_block * blocks
        self.order = [(kind, t) for t in range(main) for kind in (("mod", "main") if mod else ("main",))]


def plan():
    ph = [Phase("in1", "tok", 4, 2, 8, mod=8, k=KD, evac="z1", mod0=0),
          Phase("out1", "tok", 2, 2, 8, k=KD, evac="res")]
    for q in range(GROUPS1):
        ph.append(Phase(f"up1_{q}", "feat", 2, 2, 8, mod=8, evac="up1", mod0=8 + 4 * q))
        ph.append(Phase(f"dn1_{q}", "tok", 2, 2, 8, k=16, evac="res"))
    ph.append(Phase("inC", "tok", 3, 2, 8, k=KD, evac="zc", dest=6))
    ph.append(Phase("inL", "tok", 6, 2, 8, k=KD, evac="zl"))
    ph.append(Phase("out2", "tok", 2, 2, 8, k=KD, evac="gres"))
    for g, n in enumerate(GROUP2):
        full = n // 4 * 2 // 2
        if n % 4 == 0:
            ph.append(Phase(f"up2_{g}", "feat", n // 4, 2, 8, evac="up2", dest=0))
            ph.append(Phase(f"dn2_{g}", "tok", 2, 2, 8, k=n, evac="gres"))
        else:
            ph.append(Phase(f"up2_{g}", "feat", n // 4, 2, 8, evac="up2", dest=0))
            rest = n - 4 * (n // 4)
            if rest >= 2:
                ph.append(Phase(f"up2_{g}b", "feat", 1, 1, 8, evac="up2", dest=4 * (n // 4)))
            if rest % 2:
                ph.append(Phase(f"up2_{g}c", "feat", 1, 1, 4, evac="up2", dest=n - 1))
            ph.append(Phase(f"dn2_{g}", "tok", 1, 4, (n + 1) // 2, k=n, evac="gres"))
    seq = blk = 0
    for p in ph:
        p.seq0, p.blk0 = seq, blk
        seq += p.per_iter * p.iters
        blk += p.blocks * p.iters
    return ph


class Chain:

    def __init__(self, eng, sem, base=0):
        self.eng, self.sem, self.base, self.k = eng, sem, base, 0

    def link(self, ins):
        self.k += 1
        ins.then_inc(self.sem, 1)
        self.eng.wait_ge(self.sem, self.base + self.k)


def turns(eng, n, body):
    body(0)
    if n > 1:
        with eng.Fori(1, n) as i:
            body(i)


def program(nc, t_in, out):
    PH = plan()
    BY = {p.name: p for p in PH}
    ctx = ExitStack()
    with ctx:
        cur = [16512]

        def at(name, shape, dt, offset=None):
            size = int(np.prod(shape[1:])) * (1 if dt == U8 else 4)
            if offset is None:
                offset = cur[0]
                cur[0] += (size + 63) // 64 * 64
                assert cur[0] <= 229344, (name, cur[0])
            return nc.alloc_sbuf_tensor_at(name, shape, dt, offset=offset)

        ring0 = cur[0]
        raw = at("raw", [P, SLOTS, TW], F32)
        wlo = at("wlo", [P, SLOTS, TW], F32R, ring0)
        whi = at("whi", [P, SLOTS, TW], F32R)
        u0 = cur[0]
        uhi = at("uhi", [P, KD, TOK], F32R)
        ulo = at("ulo", [P, KD, TOK], F32R)
        h = at("h", [P, TC, D], F32)
        ca = at("ca", [P, NA], F32)
        vec = at("vec", [P, NV], F32)
        modT = at("modT", [P, NMODCH, 2], F32)
        colA = at("colA", [P, 6, KD], F32)
        stat = at("stat", [P, 8, 4], F32)
        astat = at("astat", [P, NH, 8], F32)
        bgate = at("bgate", [P, 16], F32)
        levels = at("levels", [P, 2 * LEVELS * P], U8)
        Z = cur[0]
        K = 1024

        def z_at(name, shape, dt, off, in_u=False):
            size = int(np.prod(shape[1:])) * 4
            if in_u:
                assert off + size <= 32 * K
                return at(name, shape, dt, u0 + off)
            assert Z + off + size <= 229344, (name, Z + off + size - 229344)
            return at(name, shape, dt, Z + off)

        z1 = z_at("z1", [P, TC, 4096], F32, 0)
        cb = z_at("cb", [P, NB_], F32, 32 * K)
        wf = z_at("wf", [P, NG, 2, 256], F32, 44 * K)
        cst = z_at("cst", [P, KD, P], F32R, 52 * K)
        AB = z_at("AB", [P, 2, 2, 512], F32, 60 * K)
        lev_in = z_at("lev_in", [P, 2 * LEVELS * P], F32, 60 * K)
        re = z_at("re", [P, 2, TOK], F32, 68 * K)
        qk = z_at("qk", [P, 2, 512], F32, 70 * K)
        bias = z_at("bias", [P, 512], F32, 74 * K)
        lg = z_at("lg", [P, 2, TC, TOK], F32, 76 * K)
        pT = z_at("pT", [P, 2, 2, TOK], F32, 80 * K)
        xn = z_at("xn", [P, TC, D], F32, 0)
        tpv = z_at("tpv", [P, 2, 512], F32, 24 * K)
        tpy = z_at("tpy", [P, 2, 512], F32, 48 * K)
        ahi = z_at("ahi", [P, 16, TOK], F32R, 0)
        alo = z_at("alo", [P, 16, TOK], F32R, 16 * K)
        rl = z_at("rl", [P, 1024], F32, 68 * K)
        sq = z_at("sq", [P, 1024], F32, 72 * K)
        modrow = z_at("modrow", [P, 512], F32, 76 * K)
        csilu = z_at("csilu", [P, 2, KD], F32, 80 * K)
        gfin = z_at("gfin", [P, D], F32, 40 * K)
        xc = z_at("xc", [P, TC, D], F32, 32 * K)
        zc = z_at("zc", [P, TC, 6, 512], F32, 0)
        zl = z_at("zl", [P, TC, 12, 512], F32, 0)
        LA = z_at("LA", [P, 2064], F32, 48 * K)
        WK = z_at("WK", [P, 4, 512], F32, 24 * K)
        KE = z_at("KE", [P, 4, 512], F32, 32 * K)
        S0 = z_at("S0", [P, 2, H, DV], F32, 57 * K)
        CN = z_at("CN", [P, 2, H, 258], F32, 65 * K)
        wsr = z_at("wsr", [P, KD, 32], F32, 60 * K)
        wsh = z_at("wsh", [P, KD, 32], F32R, 74 * K)
        wsl = z_at("wsl", [P, KD, 32], F32R, 76 * K)
        blr = z_at("blr", [P, 2, 512], F32, 78 * K)
        qB = z_at("qB", [P, 2, H, TOK], F32, 74 * K)
        gtb = z_at("gtb", [P, D], F32, 74 * K)
        small = 82 * K
        sm = z_at("sm", [P, TC, 32], F32, small)
        gm = z_at("gm", [P, TC, 2, 2, 8], F32, small + 256)
        wcol = z_at("wcol", [P, 2, TC, 8], F32, small + 512)
        ebend = z_at("ebend", [P, 2, H], F32, small + 640)
        mctx = z_at("mctx", [8, 4], F32, small + 704)
        kte = z_at("kte", [P, 512], F32, small + 768)
        gcol = z_at("gcol", [P, 2, 2, TC, 8], F32, small + 768)
        hden = z_at("hden", [P, 2, TC, 4], F32, small + 1024 + 256)
        rst = z_at("rst", [P, 4, TC, 8], F32, small + 1024 + 512)
        TM = z_at("TM", [P, 2064], F32, 0, True)
        wlr = z_at("wlr", [LR, 2, 512], F32, 9 * K, True)
        glrT = z_at("glrT", [32, TOK], F32, 13 * K, True)
        bT = z_at("bT", [P, H, TOK], F32, 0, True)
        EE = z_at("EE", [P, H, TOK], F32, 4 * K, True)
        gqT = z_at("gqT", [P, H, TOK], F32, 8 * K, True)
        gkT = z_at("gkT", [P, H, TOK], F32, 12 * K, True)
        qE = z_at("qE", [P, H, TOK], F32, 16 * K, True)
        kE = z_at("kE", [P, H, TOK], F32, 20 * K, True)
        ST = z_at("ST", [P, H, TC, P], F32, 24 * K, True)
        S1 = [z_at("S1a", [P, H, DV], F32, 28 * K, True), z_at("S1b", [P, H, DV], F32, 16 * K, True)]
        mqT = z_at("mqT", [P, H, TOK], F32, 0, True)
        mkT = z_at("mkT", [P, H, TOK], F32, 4 * K, True)
        WW = z_at("WW", [P, 2, TC, TOK], F32, 8 * K, True)
        qI = z_at("qI", [P, 2, TOK], F32, 12 * K, True)
        minmask = z_at("minmask", [P, 2, TC, TOK], F32, 14 * K, True)
        gnb = z_at("gnb", [P, 2, DV], F32, 18 * K, True)
        rows = z_at("rows", [8, 11, TOK], F32, 20 * K, True)
        sqj = z_at("sqj", [P, TC, 8, DV], F32, 57 * K)
        cv = z_at("cv", [P, 2, TOK], F32, 48 * K)
        sl = z_at("sl", [P, 2, TOK], F32, 50 * K)
        sv = z_at("sv", [P, 2, TOK], F32, 52 * K)
        gtmp = z_at("gtmp", [P, TC, 512], F32, 56 * K)
        PSA = ctx.enter_context(nc.psum_tensor("PSA", [P, 8, 512], F32))
        acc = PSA[:, 0:4, :]

        sem_names = {}

        def sem(name):
            sem_names[name] = ctx.enter_context(nc.semaphore(name))
            return sem_names[name]

        arrived = [sem(f"arrived{n}") for n in range(SLOTS)]
        hi_done, lo_done, tile_used = sem("hi_done"), sem("lo_done"), sem("tile_used")
        acc_free = sem("acc_free")
        row_done, mini_ready, mini_done = (sem(n) for n in ("row_done", "mini_ready", "mini_done"))
        u_ready = sem("u_ready")
        a_ready = sem("a_ready")
        ld = {n: sem("ld_" + n) for n in ("x", "const", "vec", "cb", "wf", "xc", "ws", "wlr", "gf", "bl", "mm", "gn", "out")}
        act_step, dve_step, evac_step = sem("act_step"), sem("dve_step"), sem("evac_step")
        c_done, silu_done = sem("c_done"), sem("silu_done")
        sumsq, varr, stdd, xn_done, tp_ready, tp_val, tp_hi = (sem(n) for n in (
            "sumsq", "varr", "stdd", "xn_done", "tp_ready", "tp_val", "tp_hi"))
        fa_ready, fa_act, fa_dve, fb_ready, fb_done, fc_ready, fc_hi, fc_lo = (sem(n) for n in (
            "fa_ready", "fa_act", "fa_dve", "fb_ready", "fb_done", "fc_ready", "fc_hi", "fc_lo"))
        qk_ready, qk_done, sc_ready, neg_max, exp_done, prob_done, pt_ready, pt_done, o_ready, o_hi, o_lo = (sem(n) for n in (
            "qk_ready", "qk_done", "sc_ready", "neg_max", "exp_done", "prob_done", "pt_ready", "pt_done", "o_ready", "o_hi", "o_lo"))
        h_final = sem("h_final")
        act_sq, a_hi, cv_done, sl_done = (sem(n) for n in ("act_sq", "a_hi", "cv_done", "sl_done"))
        blk2 = {n: sem(n) for n in (
            "ws_split", "nar_ready", "nar_done", "col_ready", "mulcol", "glr_ready", "glr_done", "dec_ready", "dec_done",
            "abs_done", "gate_done", "gm_done", "row_ready", "row_copy", "suf_ready", "suf_exp", "ke_done", "st_ready",
            "st_done", "w_arg", "w_exp", "wc_ready", "wk_done", "cn_ready", "cn_done", "gqt_ready", "gqt_act",
            "gqt_dve", "dg_ready", "dg_done", "cum_ready", "cum_done", "e_sub", "e_exp", "qe_done", "ke2_done", "lv_ready",
            "lv_done", "eb_exp", "qb_done", "kt_ready", "kt_exp", "kt_done", "s1_ready", "s1_done", "go_ready", "go_done",
            "mt_ready", "mt_act", "mt_dve", "mr_dve", "mr_exp", "mr_rev", "gc_ready", "gc_done", "bc_ready", "w_dve",
            "w_act", "qi_done", "ms_ready", "sw_done", "mo_ready", "mo_done", "ss_done", "rs_var", "rs_std", "silu_g", "ws_low",
            "y_done", "gt_ready", "gt_done", "fin_done", "zero_done", "diag_free")}
        B = blk2

        ident = ca[:, OFF_A["ident"][0]:OFF_A["ident"][0] + P]

        def cA(name):
            a, n = OFF_A[name]
            return ca[:, a:a + n]

        def cB(name):
            a, n = OFF_B[name]
            return cb[:, a:a + n]

        def v_(name):
            a, n = OFF_V[name]
            return vec[:, a:a + n]

        eps = EPS
        NORMS = ["mix", "mlp", "ctx", "lat", "y2", "n2"]
        OUTU = {"mix": "in1", "mlp": "up1_0", "ctx": "inC", "lat": "inL", "n2": "up2_0"}

        STEPS = {"gres": 1, "up2": 8}
        E0, at_ = {}, 0
        for p in PH:
            E0[p.name] = at_
            at_ += STEPS.get(p.evac, 0) * p.iters * p.blocks
        A0, at_ = {}, 0
        for p in PH:
            if p.evac == "up2":
                A0[p.name] = at_
                at_ += p.iters * p.blocks

        block = ctx.enter_context(nc.Block())

        @block.sync
        def _(sp):
            def load(dst, src, name):
                sp.dma_start(dst, src).then_inc(ld[name], 16)

            def tile(src, p, i, t):
                n = p.seq0 % SLOTS + t
                if isinstance(i, int) and p.seq0 + p.per_iter * i + t < SLOTS:
                    pass
                else:
                    sp.wait_ge(tile_used, p.seq0 + t + 1 - SLOTS + i * p.per_iter)
                w = src.shape[-1]
                sp.dma_start(raw[:, n % SLOTS, 0:w], src).then_inc(arrived[n % SLOTS], 16)

            def stream(p):
                def body(i):
                    for b in range(p.blocks):
                        for at, (kind, t) in enumerate(p.order):
                            n = (i * p.blocks + b)
                            if kind == "mod":
                                src = t_in["w_mod"][(n + p.mod0) * 8 + t]
                            elif p.evac == "z1":
                                src = t_in["w_in"][n * 8 + t]
                            elif p.name == "out1":
                                src = t_in["w_out"][n * 8 + t]
                            elif p.name == "out2":
                                src = t_in["w_out2"][n * 8 + t]
                            elif p.evac == "up1":
                                src = t_in["w_up"][int(p.name[4:]) * 32 + n * 8 + t]
                            elif p.name.startswith("dn1"):
                                src = t_in["w_down"][int(p.name[4:]) * 32 + n * 8 + t]
                            elif p.evac == "zc":
                                src = t_in["w_in2"][(n + 6) * 8 + t]
                            elif p.evac == "zl":
                                src = t_in["w_in2"][n * 8 + t]
                            elif p.evac == "up2":
                                g = int(p.name[4])
                                src = t_in["w_up2"][(g * 16 + p.dest) * 4 + n * 8 + t]
                            elif p.k == 16:
                                src = t_in["w_down2"][int(p.name[4]) * 32 + n * 8 + t]
                            else:
                                w = min(TW, p.k * NBLK - t * TW)
                                src = t_in["w_down2b"][n, :, t * TW:t * TW + w]
                            tile(src, p, i, b * p.per_block + at)
                            if isinstance(i, int) and i == 0 and b == 0 and at == LEAD - 1:
                                extra(p)
                turns(sp, p.iters, body)

            for t in range(TC):
                load(h[:, t, :], t_in["x"][t * P:(t + 1) * P, :], "x")
            load(ca[:, :], t_in["const_a"], "const")
            load(vec[:, :], t_in["vec"], "vec")
            load(cb[:, :], t_in["const_b"], "cb")
            load(wf[:, :, :, :], t_in["w_fourier"], "wf")
            load(lev_in[:, :], t_in["levels"], "cb")
            load(bgate[:, :], t_in["b_gate"].partition_broadcast(P), "cb")
            def extra(p):
                if p.name == "dn1_3":
                    load(gfin[:, :], t_in["g_final1"].partition_broadcast(P), "gf")
                if p.name == "inC":
                    sp.wait_ge(h_final, 2)
                    for t in range(TC):
                        load(xc[:, t, :], t_in["ctx"][t * P:(t + 1) * P, :], "xc")
                    load(wsr[:, :, :], t_in["w_in2_narrow"], "ws")
                    load(blr[:, :, :], t_in["b_lr"].partition_broadcast(P), "bl")
                if p.name == "inL":
                    sp.wait_ge(tile_used, BY["inL"].seq0)
                    sp.wait_ge(B["nar_ready"], 1)
                    load(wlr[:, :, :], t_in["w_lr"], "wlr")
                if p.name == "out2":
                    sp.wait_ge(tile_used, BY["out2"].seq0)
                    sp.wait_ge(B["nar_ready"], 2)
                    load(wlr[:, :, :], t_in["w_lr"], "wlr")
                    sp.wait_ge(B["go_done"], 4)
                    load(minmask[:, :, :, :], t_in["min_mask"], "mm")
                    load(gnb[:, :, :], t_in["g_heads"].partition_broadcast(P), "gn")
                if p.name == "up2_1":
                    load(gfin[:, :], t_in["g_final2"].partition_broadcast(P), "gf")

            for p in PH:
                stream(p)
            for t in range(TC):
                sp.wait_ge(B["fin_done"], t + 1)
                sp.dma_start(out[t * P:(t + 1) * P, :], h[:, t, :]).then_inc(ld["out"], 16)
            sp.wait_ge(ld["out"], 16 * TC)

        @block.tensor
        def _(pe):
            def weights(p, i, t):
                pe.wait_ge(lo_done, p.seq0 + t + 1 + i * p.per_iter)
                n = (p.seq0 + t) % SLOTS
                return whi[:, n, :], wlo[:, n, :]

            def product(dst, xh, xl, wh, wl, start, stop):
                pe.matmul(dst, xh, wh, start=start, stop=False)
                pe.matmul(dst, xh, wl, start=False, stop=False)
                return pe.matmul(dst, xl, wh, start=False, stop=stop)

            def mod_columns(mb):
                pe.wait_ge(row_done, mb + 1)
                if not (isinstance(mb, int) and mb == 0):
                    pe.wait_ge(mini_done, mb)
                for c in range(4):
                    mm = pe.matmul(PSA[:, 5, 2 * c:2 * c + 2], modrow[0:4, c * P:(c + 1) * P], cA("sel4")[0:4, 0:2], start=True, stop=True)
                mm.then_inc(mini_ready, 1)

            def stream(p, u0=None, a0=None, before=None):
                def body(i):
                    first = isinstance(i, int) and i == 0
                    for b in range(p.blocks):
                        nblk = p.blk0 + b + i * p.blocks
                        buf = b % 2 if p.blocks % 2 == 0 else p.blk0 % 2
                        new = first and b == 0
                        for at, (kind, t) in enumerate(p.order):
                            if kind == "mod":
                                mb = p.mod0 + b + i * p.blocks
                                if t == 0 and not (isinstance(mb, int) and mb < 2):
                                    pe.wait_ge(row_done, mb - 1)
                                wh, wl = weights(p, i, b * p.per_block + at)
                                for kk in range(2):
                                    k = 2 * t + kk
                                    lhs = cst[:, k, :]
                                    pe.matmul(PSA[:, 4 + 2 * (b % 2), :], lhs, wh[:, kk * 512:kk * 512 + 512], start=k == 0, stop=False)
                                    mm = pe.matmul(PSA[:, 4 + 2 * (b % 2), :], lhs, wl[:, kk * 512:kk * 512 + 512], start=False, stop=k == KD - 1)
                                mm.then_inc(tile_used, 1)
                            else:
                                if t == 0 and not (isinstance(nblk, int) and nblk < 2):
                                    pe.wait_ge(acc_free, nblk - 1)
                                if new and u0 is not None:
                                    if p.kind == "tok":
                                        pe.wait_ge(u_ready, u0 + t + 1)
                                    elif t < 2:
                                        pe.wait_ge(u_ready, u0 + 4 * t + 4)
                                if new and a0 is not None:
                                    per = 4 if p.name.startswith("dn1") else 2
                                    pe.wait_ge(a_ready, a0 + (min(2 * t + 2, p.k) + per - 1) // per)
                                wh, wl = weights(p, i, b * p.per_block + at)
                                if p.kind == "tok":
                                    xh, xl = (ahi, alo) if p.name.startswith("dn") else (uhi, ulo)
                                    for kk in range(2):
                                        k = 2 * t + kk
                                        if k >= p.k:
                                            continue
                                        for tt in range(TC):
                                            c = slice(kk * 512, kk * 512 + 512)
                                            s_ = slice(tt * P, (tt + 1) * P)
                                            mm = product(acc[:, 2 * buf + tt, :], xh[:, k, s_], xl[:, k, s_], wh[:, c], wl[:, c], k == 0, k == p.k - 1)
                                else:
                                    f, half = t // 2, t % 2
                                    dst = acc[:, 2 * buf + f // 2, (f % 2) * TOK:(f % 2 + 1) * TOK]
                                    for kk in range(8):
                                        k = 8 * half + kk
                                        c = slice(kk * P, (kk + 1) * P)
                                        mm = product(dst, wh[:, c], wl[:, c], uhi[:, k, :], ulo[:, k, :], k == 0, k == KD - 1)
                                mm.then_inc(tile_used, 1)
                            if at == 3:
                                if p.mod and not new:
                                    mod_columns(p.mod0 + b - 1 + i * p.blocks)
                                if new and before is not None:
                                    mod_columns(before.mod0 + before.iters * before.blocks - 1)
                turns(pe, p.iters, body)

            def norm_transposes(j):
                pe.wait_ge(xn_done, 2 * [0, 1, 2, 3, None, 4][j] + 2) if j != 4 else pe.wait_ge(B["y_done"], 4)
                for n in range(8):
                    if n >= 4 or j > 0:
                        pe.wait_ge(tp_val, 8 * j + n - 3)
                    for kk in range(2):
                        for t in range(TC):
                            k = 2 * n + kk
                            if j == 4:
                                src = zl[:, t, 2 + k // 4, (k % 4) * P:(k % 4 + 1) * P]
                            else:
                                src = xn[:, t, k * P:(k + 1) * P]
                            mm = pe.transpose(PSA[:, 4 + n % 4, kk * TOK + t * P:kk * TOK + (t + 1) * P], src, ident)
                    mm.then_inc(tp_ready, 1)
                pe.wait_ge(tp_val, 8 * (j + 1))

            def gate_rows(first, j):
                for n in range(4):
                    pe.wait_ge(tp_val, 8 * j)
                    for c in range(4):
                        mm = pe.matmul(PSA[:, n, c * P:(c + 1) * P], modT[:, first + 4 * n + c, 0:1].broadcast_to([P, P]), ident,
                                       start=True, stop=True)
                    mm.then_inc(B["gt_ready"], 1)

            pe.wait_ge(ld["const"], 16)
            norm_transposes(0)
            pe.wait_ge(c_done, 1)
            stream(BY["in1"], u0=0)
            mod_columns(7)

            pe.wait_ge(ld["cb"], 48)
            pe.wait_ge(ld["wf"], 16)
            pe.wait_ge(acc_free, BY["out1"].blk0)
            pe.wait_ge(mini_done, 8)
            for s in range(NH + 3):
                if s < NG:
                    if s >= 1:
                        pe.wait_ge(fa_act, s)
                        pe.wait_ge(fa_dve, s)
                    for c in range(2):
                        for t in range(TC):
                            mm = pe.matmul(PSA[:, c, :], z1[:, t, s * 256 + c * P:s * 256 + (c + 1) * P],
                                           cB("dft_pos")[:, t * 512:(t + 1) * 512], start=t == 0, stop=t == 1)
                        mm.then_inc(fa_ready, 1)
                g = s - 1
                if 0 <= g < NG:
                    pe.wait_ge(fa_act, g + 1)
                    pe.wait_ge(fa_dve, g + 1)
                    if g >= 1:
                        pe.wait_ge(fb_done, g)
                    for c2 in range(2):
                        for c in range(2):
                            for m, (name, part) in enumerate((("dft_cos", 0), ("dft_nsin", 1))):
                                mm = pe.matmul(PSA[:, 2, c2 * TOK:(c2 + 1) * TOK], cB(name)[:, c * 256 + c2 * P:c * 256 + (c2 + 1) * P],
                                               AB[:, g % 2, c, part * TOK:(part + 1) * TOK], start=c == 0 and m == 0, stop=c == 1 and m == 1)
                    mm.then_inc(fb_ready, 1)
                g = s - 2
                if 0 <= g < NG:
                    pe.wait_ge(fb_done, g + 1)
                    if g >= 1:
                        pe.wait_ge(fc_hi, g)
                        pe.wait_ge(fc_lo, g)
                    for e in range(2):
                        for c in range(2):
                            mm = pe.matmul(PSA[:, 3, e * TOK:(e + 1) * TOK], wf[:, g, c, e * P:(e + 1) * P], re[:, c, :],
                                           start=c == 0, stop=c == 1)
                    mm.then_inc(fc_ready, 1)
                if s < NH:
                    if s >= 1:
                        pe.wait_ge(qk_done, s)
                    for n, c0 in enumerate((1024, 2048)):
                        for t in range(TC):
                            mm = pe.transpose(PSA[:, 4, n * TOK + t * P:n * TOK + (t + 1) * P], z1[:, t, c0 + s * DH:c0 + (s + 1) * DH], ident)
                    mm.then_inc(qk_ready, 1)
                hd = s - 1
                if 0 <= hd < NH:
                    pe.wait_ge(qk_done, hd + 1)
                    if hd >= 1:
                        pe.wait_ge(neg_max, hd)
                    for t in range(TC):
                        mm = pe.matmul(PSA[:, 5, t * TOK:(t + 1) * TOK], qk[:, hd % 2, t * P:(t + 1) * P], qk[:, hd % 2, TOK:2 * TOK],
                                       start=True, stop=True)
                    mm.then_inc(sc_ready, 1)
                hd = s - 2
                if 0 <= hd < NH:
                    pe.wait_ge(prob_done, hd + 1)
                    if hd >= 1:
                        pe.wait_ge(pt_done, hd)
                    for kc in range(TC):
                        for t in range(TC):
                            mm = pe.transpose(PSA[:, 6, kc * TOK + t * P:kc * TOK + (t + 1) * P], lg[:, hd % 2, t, kc * P:(kc + 1) * P], ident)
                    mm.then_inc(pt_ready, 1)
                hd = s - 3
                if 0 <= hd < NH:
                    pe.wait_ge(pt_done, hd + 1)
                    if hd >= 1:
                        pe.wait_ge(o_hi, hd)
                        pe.wait_ge(o_lo, hd)
                    for kc in range(TC):
                        mm = pe.matmul(PSA[:, 7, 0:TOK], z1[:, kc, 3072 + hd * DH:3072 + (hd + 1) * DH], pT[:, hd % 2, kc, :],
                                       start=kc == 0, stop=kc == 1)
                    mm.then_inc(o_ready, 1)
            pe.wait_ge(fc_lo, NG)
            pe.wait_ge(o_lo, NH)
            stream(BY["out1"])
            norm_transposes(1)
            for q in range(GROUPS1):
                stream(BY[f"up1_{q}"], u0=8 if q == 0 else None)
                stream(BY[f"dn1_{q}"], a0=4 * q, before=BY[f"up1_{q}"])
            norm_transposes(2)
            stream(BY["inC"], u0=16)

            def narrow(x):
                pe.wait_ge(B["ws_low"], 1)
                for t in range(TC):
                    for k in range(KD):
                        mm = product(PSA[:, 4, t * 32:(t + 1) * 32], uhi[:, k, t * P:(t + 1) * P], ulo[:, k, t * P:(t + 1) * P],
                                     wsh[:, k, :], wsl[:, k, :], k == 0, k == KD - 1)
                mm.then_inc(B["nar_ready"], 1)
                pe.wait_ge(B["nar_done"], x + 1)
                for t in range(TC):
                    mm = pe.transpose(PSA[0:32, 5, t * P:(t + 1) * P], sm[:, t, :], ident)
                mm.then_inc(B["glr_ready"], 1)
                pe.wait_ge(B["glr_done"], x + 1)
                pe.wait_ge(ld["wlr"], 16 * (x + 1))
                pe.wait_ge(acc_free, BY["inL" if x == 0 else "out2"].blk0)
                for t in range(TC):
                    for z in range(2):
                        mm = pe.matmul(PSA[:, 2 * t + z, :], glrT[0:LR, t * P:(t + 1) * P], wlr[:, z, :], start=True, stop=True)
                mm.then_inc(B["dec_ready"], 1)

            def gate_matrix_rows(x):
                pe.wait_ge(B["gm_done"], x + 1)
                for kind in range(2):
                    for t in range(TC):
                        dst = PSA[0:8, 6, kind * TOK + t * P:kind * TOK + (t + 1) * P]
                        pe.matmul(dst, gm[:, t, 0, kind, :], ident, start=True, stop=False)
                        mm = pe.matmul(dst, gm[:, 1 - t, 1, kind, :], cA("flip"), start=False, stop=True)
                mm.then_inc(B["row_ready"], 1)

            def LA4(t, z):
                return LA[:, (2 * t + z) * 512:(2 * t + z + 1) * 512]

            narrow(0)
            gate_matrix_rows(0)
            for z in range(2):
                for t in range(TC):
                    dst = PSA[:, 2 * z + t, :]
                    if z == 0 and t == 0:
                        pe.matmul(dst, cA("suf"), LA4(0, 0), start=True, stop=False)
                        mm = pe.matmul(dst, cA("one16"), LA4(1, 0), start=False, stop=True)
                    elif z == 0:
                        mm = pe.matmul(dst, cA("suf"), LA4(1, 0), start=True, stop=True)
                    elif t == 0:
                        mm = pe.matmul(dst, cA("pre"), LA4(0, 1), start=True, stop=True)
                    else:
                        pe.matmul(dst, cA("one16"), LA4(0, 1), start=True, stop=False)
                        mm = pe.matmul(dst, cA("pre"), LA4(1, 1), start=False, stop=True)
            mm.then_inc(B["suf_ready"], 1)
            pe.wait_ge(B["mr_rev"], 1)
            for z in range(2):
                for t in range(TC):
                    mm = pe.transpose(PSA[:, 7, (2 * z + t) * 8:(2 * z + t + 1) * 8], rows[:, 5 + z, t * P:(t + 1) * P], ident[0:8, 0:8])
            mm.then_inc(B["wc_ready"], 1)
            pe.wait_ge(B["ke_done"], 4)
            for z in range(2):
                for h2 in range(2):
                    for hh in range(2):
                        hd = 2 * h2 + hh
                        for t in range(TC):
                            mm = pe.matmul(PSA[:, 2 * z + h2, hh * DV:(hh + 1) * DV], KE[:, 2 * z + t, hd * DK:(hd + 1) * DK],
                                           zc[:, t, 2 + h2, hh * DV:(hh + 1) * DV], start=t == 0, stop=t == 1)
                    mm.then_inc(B["st_ready"], 1)
            pe.wait_ge(B["wk_done"], 4)
            for n in range(8):
                z, hd = n // 4, n % 4
                if n >= 2:
                    pe.wait_ge(B["cn_done"], n - 1)
                for t in range(TC):
                    pe.matmul(PSA[:, 4 + n % 2, 0:DV], WK[:, 2 * z + t, hd * DK:(hd + 1) * DK],
                              zc[:, t, 4 + hd // 2, (hd % 2) * DV:(hd % 2 + 1) * DV], start=t == 0, stop=t == 1)
                for t in range(TC):
                    mm = pe.matmul(PSA[:, 4 + n % 2, DV:DV + 2], WK[:, 2 * z + t, hd * DK:(hd + 1) * DK], cA("ones")[:, 0:2],
                                   start=t == 0, stop=t == 1)
                mm.then_inc(B["cn_ready"], 1)
            pe.wait_ge(B["cn_done"], 8)
            pe.wait_ge(B["st_done"], 4)

            norm_transposes(3)
            stream(BY["inL"], u0=24)
            narrow(1)
            pe.wait_ge(B["gm_done"], 2)

            pe.wait_ge(acc_free, BY["out2"].blk0)
            for n, blk in enumerate((0, 6)):
                for hd in range(H):
                    for t in range(TC):
                        mm = pe.transpose(PSA[:, 2 * n + hd // 2, (hd % 2) * TOK + t * P:(hd % 2) * TOK + (t + 1) * P],
                                          zl[:, t, blk, hd * DK:(hd + 1) * DK], ident)
                mm.then_inc(B["gqt_ready"], 1)

            def scores(lq, lk, b0):
                for hd in range(H):
                    for t in range(TC):
                        c = hd * TC + t
                        mm = pe.matmul(PSA[:, b0 + c // 4, (c % 4) * P:(c % 4 + 1) * P], lk[:, hd, t * P:(t + 1) * P],
                                       lq[:, hd, t * P:(t + 1) * P], start=True, stop=True)
                return mm

            pe.wait_ge(B["gqt_act"], 1)
            pe.wait_ge(B["gqt_dve"], 1)
            scores(gqT, gkT, 4).then_inc(B["dg_ready"], 1)
            for z in range(2):
                if z:
                    pe.wait_ge(B["cum_done"], 1)
                for hd in range(H):
                    for t in range(TC):
                        mm = pe.matmul(PSA[:, hd // 2, (hd % 2) * TOK + t * P:(hd % 2) * TOK + (t + 1) * P],
                                       LA4(t, z)[:, hd * DK:(hd + 1) * DK], cA("inc_b" if z else "inc_f"), start=True, stop=True)
                mm.then_inc(B["cum_ready"], 1)
                for n in range(LEVELS):
                    m = z * LEVELS + n
                    pe.wait_ge(B["qe_done"], m + 1)
                    pe.wait_ge(B["ke2_done"], m + 1)
                    if m >= 2:
                        pe.wait_ge(B["lv_done"], m - 1)
                    scores(qE, kE, 2 if m % 2 else 6).then_inc(B["lv_ready"], 1)
                pe.wait_ge(B["dg_done"], 1)
                if z:
                    pe.wait_ge(B["s1_done"], 1)
                pe.matmul(PSA[:, 4, :], cA("pre" if z else "suf"), LA4(z, z), start=True, stop=True).then_inc(B["kt_ready"], 1)
                pe.wait_ge(B["kt_done"], z + 1)
                pe.wait_ge(B["cum_done"], z + 1)
                for hd in range(H):
                    mm = pe.matmul(PSA[:, hd // 2, (hd % 2) * DV:(hd % 2 + 1) * DV], kte[:, hd * DK:(hd + 1) * DK],
                                   zl[:, z, 8 + hd // 2, (hd % 2) * DV:(hd % 2 + 1) * DV], start=True, stop=True)
                mm.then_inc(B["s1_ready"], 1)
                pe.wait_ge(B["s1_done"], z + 1)
            pe.wait_ge(B["lv_done"], 2 * LEVELS)
            pe.wait_ge(B["qb_done"], 2)
            for t in range(TC):
                for h2 in range(2):
                    for hh in range(2):
                        hd = 2 * h2 + hh
                        dst = PSA[:, 4 + 2 * t + h2, hh * DV:(hh + 1) * DV]
                        pe.matmul(dst, ST[:, hd, t, :], zl[:, t, 8 + h2, hh * DV:(hh + 1) * DV], start=True, stop=False)
                        pe.matmul(dst, qB[:, 0, hd, t * P:(t + 1) * P], (S1[0][:, hd, :] if t else S0[:, 0, hd, :]), start=False, stop=False)
                        mm = pe.matmul(dst, qB[:, 1, hd, t * P:(t + 1) * P], (S0[:, 1, hd, :] if t else S1[1][:, hd, :]), start=False, stop=True)
                    mm.then_inc(B["go_ready"], 1)

            for n, blk in enumerate((1, 7)):
                for hd in range(H):
                    for t in range(TC):
                        mm = pe.transpose(PSA[:, 2 * n + hd // 2, (hd % 2) * TOK + t * P:(hd % 2) * TOK + (t + 1) * P],
                                          zl[:, t, blk, hd * DK:(hd + 1) * DK], ident)
                mm.then_inc(B["mt_ready"], 1)
            pe.wait_ge(B["go_done"], 4)
            gate_matrix_rows(1)
            pe.wait_ge(B["mr_rev"], 2)
            for w in range(2):
                for z in range(2):
                    for t in range(TC):
                        c = ((w * 2 + z) * TC + t) * 8
                        mm = pe.transpose(PSA[:, 4, c:c + 8], rows[:, (5 if w == 0 else 7) + z, t * P:(t + 1) * P], ident[0:8, 0:8])
            mm.then_inc(B["gc_ready"], 1)
            pe.wait_ge(B["mt_act"], 1)
            pe.wait_ge(B["mt_dve"], 1)
            pe.wait_ge(B["gc_done"], 1)
            for s in range(9):
                if s < 8:
                    z, hd = s // 4, s % 4
                    if s >= 2:
                        pe.wait_ge(B["w_dve"], s - 1)
                        pe.wait_ge(B["qi_done"], s - 1)
                    src = rows[:, 9:11, ::-1] if z else rows[:, 9:11, :]
                    pe.matmul(PSA[:, s % 2, :], ident[0:8, s:s + 1].broadcast_to([8, P]), src, start=True, stop=True).then_inc(B["bc_ready"], 1)
                    if s >= 2:
                        pe.wait_ge(B["sw_done"], s - 1)
                    for t in range(TC):
                        mm = pe.matmul(PSA[:, 2 + s % 2, t * TOK:(t + 1) * TOK], mkT[:, hd, t * P:(t + 1) * P], mqT[:, hd, :], start=True, stop=True)
                    mm.then_inc(B["ms_ready"], 1)
                if s >= 1:
                    r = s - 1
                    z, hd = r // 4, r % 4
                    pe.wait_ge(B["sw_done"], r + 1)
                    if r >= 2:
                        pe.wait_ge(B["mo_done"], r - 1)
                    for jc in range(TC):
                        dst = PSA[:, 4 + 2 * (r % 2) + jc, :]
                        ts_ = [t for t in range(TC) if (t <= jc if z == 0 else t >= jc)]
                        for part in range(2):
                            for n, t in enumerate(ts_):
                                rhs = zl[:, t, 10 + hd // 2, (hd % 2) * DV:(hd % 2 + 1) * DV] if part == 0 else cA("ones")[:, 0:2]
                                c = slice(0, DV) if part == 0 else slice(DV, DV + 2)
                                pe.matmul(dst[:, c], WW[:, r % 2, t, jc * P:(jc + 1) * P], rhs, start=n == 0, stop=False)
                            mm = pe.matmul(dst[:, c], qI[:, r % 2, jc * P:(jc + 1) * P], CN[:, z, hd, c], start=False, stop=True)
                    mm.then_inc(B["mo_ready"], 1)
            pe.wait_ge(B["mo_done"], 8)
            norm_transposes(4)
            gate_rows(2 * KD, 5)
            pe.wait_ge(B["gt_done"], 1)
            stream(BY["out2"], u0=32)
            norm_transposes(5)
            gate_rows(5 * KD, 6)
            pe.wait_ge(B["gt_done"], 2)
            for g in range(len(GROUP2)):
                for p in PH:
                    if p.name.startswith(f"up2_{g}"):
                        stream(p, u0=40 if p.name == "up2_0" else None)
                stream(BY[f"dn2_{g}"], a0=4 * GROUPS1 + 8 * g)

        @block.scalar
        def _(act):
            ch = Chain(act, act_step)
            AF = act.activation

            def evacuate(p, i, b):
                end = p.seq0 + (b + 1) * p.per_block + i * p.per_iter
                nb = i * p.blocks + b
                buf = (b % 2) if p.blocks % 2 == 0 else p.blk0 % 2
                if p.mod:
                    mb = p.mod0 + nb
                    act.wait_ge(tile_used, end)
                    if not (isinstance(mb, int) and mb == 0):
                        act.wait_ge(mini_ready, mb)
                    AF(modrow[0:4, :], PSA[0:4, 4 + 2 * (b % 2), :], ACT.Copy).then_inc(row_done, 1)
                if p.evac in ("z1", "zc", "zl"):
                    act.wait_ge(tile_used, end)
                    z = {"z1": z1[:, :, :].rearrange("p t (n c) -> p t n c", c=512), "zc": zc, "zl": zl}[p.evac]
                    AF(z[:, 0, nb, :], acc[:, 2 * buf, :], ACT.Copy)
                    AF(z[:, 1, nb, :], acc[:, 2 * buf + 1, :], ACT.Copy).then_inc(acc_free, 1)
                if p.evac == "up1":
                    ab = int(p.name[4]) * 4 + nb + 1
                    act.wait_ge(acc_free, p.blk0 + nb + 1)
                    AF(sq[:, :], rl[:, :], ACT.Square).then_inc(act_sq, 1)
                    act.wait_ge(act_sq, ab)
                    AF(ahi[:, :, :].rearrange("p (n f) t -> p n (f t)", f=4)[:, nb, :], sq[:, :], ACT.Copy).then_inc(a_hi, 1)
                if p.evac == "up2":
                    ab = nb + 1 + A0[p.name]
                    w = 2 if p.main == 8 else 1
                    act.wait_ge(cv_done, ab)
                    AF(sl[:, 0:w, :], cv[:, 0:w, :], ACT.Silu).then_inc(sl_done, 1)
                    act.wait_ge(acc_free, p.blk0 + nb + 1)
                    if w == 2:
                        dst = ahi[:, :, :].rearrange("p (n f) t -> p n f t", f=2)[:, nb + p.dest // 2, :, :]
                    else:
                        dst = ahi[:, p.dest:p.dest + 1, :]
                    AF(dst, sv[:, 0:w, :], ACT.Copy).then_inc(a_hi, 1)

            def split(p, i, t):
                n = p.seq0 + t
                w = TW
                if p.k == 11 and (t % p.per_block) == p.per_block - 1:
                    w = NBLK
                act.wait_ge(arrived[n % SLOTS], 16 * (n // SLOTS + 1) + i * (2 * p.per_iter))
                AF(whi[:, n % SLOTS, 0:w], raw[:, n % SLOTS, 0:w], ACT.Copy).then_inc(hi_done, 1)

            def stream(p, flush):
                def body(i):
                    for b in range(p.blocks):
                        for t in range(p.per_block):
                            split(p, i, b * p.per_block + t)
                            if t == LEAD - 1:
                                if b > 0:
                                    evacuate(p, i, b - 1)
                                elif isinstance(i, int) and i == 0:
                                    flush()
                                else:
                                    evacuate(p, i - 1, p.blocks - 1)
                turns(act, p.iters, body)

            def sum_squares(s, src, free):
                free()
                for t in range(TC):
                    AF(xn[:, t, :], src[:, t, :], ACT.Square, accum_out=stat[:, s, t:t + 1]).then_inc(sumsq, 1)
                act.wait_ge(varr, s + 1)
                AF(stat[:, s, 2:4], stat[:, s, 0:2], ACT.Sqrt).then_inc(stdd, 1)

            def transposes_hi(j):
                buf = tpy if j == 4 else tpv
                for n in range(8):
                    act.wait_ge(tp_val, 8 * j + n + 1)
                    AF(uhi[:, 2 * n:2 * n + 2, :], buf[:, n % 2, :], ACT.Copy).then_inc(tp_hi, 1)

            def start():
                act.wait_ge(ld["vec"], 16)
                AF(csilu[:, :, :], vec[:, OFF_V["c"][0]:OFF_V["c"][0] + 2 * KD], ACT.Silu).then_inc(silu_done, 1)
                sum_squares(0, h, lambda: act.wait_ge(ld["x"], 32))
                transposes_hi(0)

            def mix1():
                for s in range(NH + 3):
                    if s < NG:
                        act.wait_ge(fa_ready, 2 * s + 1)
                        if s >= 2:
                            act.wait_ge(fb_ready, s - 1)
                        AF(AB[:, s % 2, 0, :], PSA[:, 0, :], ACT.Copy).then_inc(fa_act, 1)
                    g = s - 1
                    if 0 <= g < NG:
                        act.wait_ge(fb_ready, g + 1)
                        if g >= 1:
                            act.wait_ge(fc_ready, g)
                        AF(re[:, :, :], PSA[:, 2, :], ACT.Copy).then_inc(fb_done, 1)
                    g = s - 2
                    if 0 <= g < NG:
                        act.wait_ge(fc_ready, g + 1)
                        AF(uhi[:, 2 * g:2 * g + 2, :], PSA[:, 3, :], ACT.Copy).then_inc(fc_hi, 1)
                    if s < NH:
                        act.wait_ge(qk_ready, s + 1)
                        if s >= 2:
                            act.wait_ge(sc_ready, s - 1)
                        AF(qk[:, s % 2, :], PSA[:, 4, :], ACT.Copy).then_inc(qk_done, 1)
                    hd = s - 1
                    if 0 <= hd < NH:
                        act.wait_ge(neg_max, hd + 1)
                        for t in range(TC):
                            AF(lg[:, hd % 2, t, :], lg[:, hd % 2, t, :], ACT.Exp, bias=astat[:, hd, t:t + 1],
                               accum_out=astat[:, hd, 2 + t:3 + t]).then_inc(exp_done, 1)
                    hd = s - 2
                    if 0 <= hd < NH:
                        act.wait_ge(pt_ready, hd + 1)
                        if hd >= 2:
                            act.wait_ge(o_ready, hd - 1)
                        AF(pT[:, hd % 2, :, :], PSA[:, 6, :], ACT.Copy).then_inc(pt_done, 1)
                    hd = s - 3
                    if 0 <= hd < NH:
                        act.wait_ge(o_ready, hd + 1)
                        AF(uhi[:, 8 + hd, :], PSA[:, 7, 0:TOK], ACT.Copy).then_inc(o_hi, 1)

            def norm(j, s, src, n_blocks, other=None):
                def free():
                    act.wait_ge(acc_free, n_blocks)
                    if other is not None:
                        other()
                sum_squares(s, src, free)
                transposes_hi(j)

            def context():
                sum_squares(2, h, lambda: act.wait_ge(acc_free, BY["inC"].blk0))
                norm(2, 3, xc, BY["inC"].blk0, lambda: (act.wait_ge(ld["xc"], 32), act.wait_ge(h_final, 2)))
                act.wait_ge(ld["ws"], 16)
                AF(wsh[:, :, :], wsr[:, :, :], ACT.Copy).then_inc(B["ws_split"], 1)

            def gates(x):
                act.wait_ge(B["glr_ready"], x + 1)
                AF(glrT[:, :], PSA[0:32, 5, 0:TOK], ACT.Copy).then_inc(B["glr_done"], 1)
                act.wait_ge(B["dec_done"], x + 1)
                ch.link(AF(TM[:, :], LA[:, :], ACT.Abs))
                ch.link(AF(TM[:, :], TM[:, :], ACT.Exp, scale=-1.0))
                AF(TM[:, :], TM[:, :], ACT.Ln, bias=1.0).then_inc(B["abs_done"], 1)

            def context_states():
                gates(0)
                act.wait_ge(B["suf_ready"], 1)
                for n in range(4):
                    AF(KE[:, n, :], PSA[:, n, :], ACT.Exp).then_inc(B["suf_exp"], 1)
                act.wait_ge(B["w_arg"], 1)
                AF(rows[:, 5, :], rows[:, 4, :], ACT.Exp, bias=mctx[:, 1:2]).then_inc(B["mr_exp"], 1)
                for n in range(4):
                    act.wait_ge(B["st_ready"], n + 1)
                    AF(S0[:, n // 2, 2 * (n % 2):2 * (n % 2) + 2, :], PSA[:, n, :], ACT.Copy).then_inc(B["st_done"], 1)
                for n in range(8):
                    act.wait_ge(B["cn_ready"], n + 1)
                    AF(CN[:, n // 4, n % 4, :], PSA[:, 4 + n % 2, 0:DV + 2], ACT.Copy).then_inc(B["cn_done"], 1)
                sum_squares(4, h, lambda: None)
                transposes_hi(3)

            def heads2():
                gates(1)
                act.wait_ge(B["gate_done"], 2)
                act.wait_ge(B["gqt_ready"], 1)
                AF(gqT[:, :, :], PSA[:, 0:2, :], ACT.Copy, scale=DK ** -0.5).then_inc(B["gqt_act"], 1)
                for z in range(2):
                    act.wait_ge(B["cum_ready"], z + 1)
                    if z:
                        act.wait_ge(B["qb_done"], 1)
                    AF(bT[:, :, :], PSA[:, 0:2, :], ACT.Copy).then_inc(B["cum_done"], 1)
                    for n in range(LEVELS):
                        m = z * LEVELS + n
                        act.wait_ge(B["e_sub"], m + 1)
                        ch.link(AF(EE[:, :, :], EE[:, :, :], ACT.Abs))
                        AF(EE[:, :, :], EE[:, :, :], ACT.Exp, scale=-1.0).then_inc(B["e_exp"], 1)
                    act.wait_ge(B["qe_done"], (z + 1) * LEVELS)
                    act.wait_ge(B["ke2_done"], (z + 1) * LEVELS)
                    AF(EE[:, :, :], bT[:, :, :], ACT.Exp).then_inc(B["eb_exp"], 1)
                    act.wait_ge(B["kt_ready"], z + 1)
                    AF(kte[:, :], PSA[:, 4, :], ACT.Exp).then_inc(B["kt_exp"], 1)
                for n in range(4):
                    act.wait_ge(B["go_ready"], n + 1)
                    AF(zl[:, n // 2, 6 * (n % 2), :], PSA[:, 4 + n, :], ACT.Copy).then_inc(B["go_done"], 1)
                act.wait_ge(B["mt_ready"], 1)
                act.wait_ge(B["qb_done"], 2)
                AF(mqT[:, :, :], PSA[:, 0:2, :], ACT.Copy).then_inc(B["mt_act"], 1)
                for t in range(TC):
                    AF(zl[:, t, 2:4, :], zl[:, t, 2:4, :], ACT.Silu).then_inc(B["silu_g"], 1)
                for t in range(TC):
                    AF(zl[:, t, 4:6, :], zl[:, t, 4:6, :], ACT.Sigmoid).then_inc(B["silu_g"], 1)
                act.wait_ge(B["w_arg"], 2)
                AF(rows[:, 7, :], rows[:, 8, :], ACT.Exp, scale=-1.0)
                AF(rows[:, 10, :], rows[:, 9, :], ACT.Exp, bias=mctx[:, 0:1]).then_inc(B["mr_exp"], 1)
                for s in range(8):
                    act.wait_ge(B["w_dve"], s + 1)
                    AF(WW[:, s % 2, :, :], WW[:, s % 2, :, :], ACT.Exp).then_inc(B["w_act"], 1)
                act.wait_ge(B["mo_done"], 8)
                for t in range(TC):
                    for n in range(8):
                        blk = (0, 6, 1, 7)[n // 2]
                        AF(sqj[:, t, n, :], zl[:, t, blk, (n % 2) * DV:(n % 2 + 1) * DV], ACT.Square,
                           accum_out=rst[:, 0, t, n:n + 1]).then_inc(B["ss_done"], 1)
                act.wait_ge(B["rs_var"], 1)
                AF(rst[:, 1, :, :], rst[:, 0, :, :], ACT.Sqrt).then_inc(B["rs_std"], 1)
                transposes_hi(4)

            interlude = {"in1": mix1, "out1": lambda: norm(1, 1, h, BY["up1_0"].blk0), "dn1_3": context,
                         "inC": context_states, "inL": heads2,
                         "out2": lambda: norm(5, 5, h, BY["up2_0"].blk0)}
            flush = start
            for p in PH:
                stream(p, flush)

                def flush(p=p):
                    evacuate(p, p.iters - 1, p.blocks - 1)
                    if p.name in interlude:
                        interlude[p.name]()
            sum_squares(6, h, lambda: act.wait_ge(acc_free, BY["dn2_2"].blk0 + 4))

        @block.vector
        def _(dve):
            ch = Chain(dve, dve_step)

            def mod_add(mb):
                dve.wait_ge(mini_ready, mb + 1)
                bm = v_("b_mod").rearrange("p (n c) -> p n c", c=4)[:, mb, :]
                TT(modT[:, :, :].rearrange("p (n c) w -> p n c w", c=4)[:, mb, :, :],
                   PSA[:, 5, 0:8].rearrange("p (c w) -> p c w", w=2), bm.unsqueeze(2).broadcast_to([P, 4, 2]), ALU.add).then_inc(mini_done, 1)

            TT, TS, STT, CP = dve.tensor_tensor, dve.tensor_scalar, dve.scalar_tensor_tensor, dve.tensor_copy

            def evacuate(p, i, b):
                end = p.seq0 + (b + 1) * p.per_block + i * p.per_iter
                nb = i * p.blocks + b
                ch = Chain(dve, evac_step, E0[p.name] + STEPS.get(p.evac, 0) * nb)
                buf = (b % 2) if p.blocks % 2 == 0 else p.blk0 % 2
                if p.evac == "res":
                    dve.wait_ge(tile_used, end)
                    hb = h[:, :, :].rearrange("p t (n c) -> p t n c", c=512)[:, :, nb, :]
                    TT(hb, acc[:, 2 * buf:2 * buf + 2, :], hb, ALU.add).then_inc(acc_free, 1)
                if p.evac == "gres":
                    dve.wait_ge(tile_used, end)
                    hb = h[:, :, :].rearrange("p t (n c) -> p t n c", c=512)[:, :, nb, :]
                    gb = gtb[:, :].rearrange("p (n c) -> p n c", c=512)[:, nb, :]
                    for t in range(TC):
                        ins = TT(gtmp[:, t, :], acc[:, 2 * buf + t, :], gb, ALU.mult)
                    ch.link(ins)
                    TT(hb, gtmp[:, :, :], hb, ALU.add).then_inc(acc_free, 1)
                if p.evac == "up1":
                    ab = int(p.name[4]) * 4 + nb + 1
                    dve.wait_ge(tile_used, end)
                    TS(rl[:, :], acc[:, 2 * buf:2 * buf + 2, :], 0.0, None, ALU.max).then_inc(acc_free, 1)
                    dve.wait_ge(a_hi, ab)
                    f4 = "p (n f) t -> p n (f t)"
                    TT(alo[:, :, :].rearrange(f4, f=4)[:, nb, :], sq[:, :], ahi[:, :, :].rearrange(f4, f=4)[:, nb, :],
                       ALU.subtract).then_inc(a_ready, 1)
                if p.evac == "up2":
                    ab = nb + 1 + A0[p.name]
                    w = 2 if p.main == 8 else 1
                    dve.wait_ge(tile_used, end)
                    ck = int(p.name[4]) * 16 + p.dest + i * (2 * p.blocks) + 2 * b
                    cwv = v_("conv_w").rearrange("p (n k) -> p n k", k=9)
                    cbv = v_("conv_b").rearrange("p (n k) -> p n k", k=1)
                    gate = [acc[:, 2 * buf + n, 0:TOK].rearrange("p (r c) -> p r c", c=64) for n in range(w)]
                    cvv = [cv[:, n, :].rearrange("p (r c) -> p r c", c=64) for n in range(w)]
                    for n in range(w):
                        last = TS(cvv[n], gate[n], cwv[:, ck + n, 4:5], cbv[:, ck + n, :], ALU.mult, ALU.add)
                    ch.link(last)
                    for tap in (0, 1, 2, 3, 5, 6, 7, 8):
                        dr, dc = tap // 3 - 1, tap % 3 - 1
                        ro = slice(max(0, -dr), 4 - max(0, dr))
                        ri = slice(max(0, dr), 4 + min(0, dr))
                        co = slice(max(0, -dc), 64 - max(0, dc))
                        ci = slice(max(0, dc), 64 + min(0, dc))
                        for n in range(w):
                            last = STT(cvv[n][:, ro, co], gate[n][:, ri, ci], cwv[:, ck + n, tap:tap + 1], cvv[n][:, ro, co], ALU.mult, ALU.add)
                        if tap < 8:
                            ch.link(last)
                        else:
                            last.then_inc(cv_done, 1)
                    dve.wait_ge(sl_done, ab)
                    TT(sv[:, 0:w, :], acc[:, 2 * buf:2 * buf + w, TOK:2 * TOK], sl[:, 0:w, :], ALU.mult).then_inc(acc_free, 1)
                    dve.wait_ge(a_hi, 4 * GROUPS1 + ab)
                    if w == 2:
                        f2 = "p (n f) t -> p n f t"
                        dh = ahi[:, :, :].rearrange(f2, f=2)[:, nb + p.dest // 2, :, :]
                        dl = alo[:, :, :].rearrange(f2, f=2)[:, nb + p.dest // 2, :, :]
                    else:
                        dh, dl = ahi[:, p.dest:p.dest + 1, :], alo[:, p.dest:p.dest + 1, :]
                    TT(dl, sv[:, 0:w, :], dh, ALU.subtract).then_inc(a_ready, 1)

            def split(p, i, t):
                n = p.seq0 + t
                w = TW
                if p.k == 11 and (t % p.per_block) == p.per_block - 1:
                    w = NBLK
                dve.wait_ge(hi_done, n + 1 + i * p.per_iter)
                TT(wlo[:, n % SLOTS, 0:w], raw[:, n % SLOTS, 0:w], whi[:, n % SLOTS, 0:w], ALU.subtract).then_inc(lo_done, 1)

            def stream(p, flush, before):
                def body(i):
                    for b in range(p.blocks):
                        for t in range(p.per_block):
                            split(p, i, b * p.per_block + t)
                            if t == 7:
                                new = b == 0 and isinstance(i, int) and i == 0
                                if p.mod and not new:
                                    mod_add(p.mod0 + b - 1 + i * p.blocks)
                                if new and before is not None:
                                    mod_add(before.mod0 + before.iters * before.blocks - 1)
                            if t == LEAD - 1:
                                if b > 0:
                                    evacuate(p, i, b - 1)
                                elif isinstance(i, int) and i == 0:
                                    flush()
                                else:
                                    evacuate(p, i - 1, p.blocks - 1)
                turns(dve, p.iters, body)

            def variance(s, width=D):
                dve.wait_ge(sumsq, 2 * (s + 1))
                TS(stat[:, s, 0:2], stat[:, s, 0:2], 1.0 / width, eps, ALU.mult, ALU.add).then_inc(varr, 1)
                dve.wait_ge(stdd, s + 1)
                ch.link(dve.reciprocal(stat[:, s, 2:4], stat[:, s, 2:4]))

            def transposes_lo(j, A, Bc):
                buf = tpy if j == 4 else tpv

                def low(n):
                    dve.wait_ge(tp_hi, 8 * j + n + 1)
                    TT(ulo[:, 2 * n:2 * n + 2, :], buf[:, n % 2, :].rearrange("p (k t) -> p k t", k=2), uhi[:, 2 * n:2 * n + 2, :],
                       ALU.subtract).then_inc(u_ready, 1)
                for n in range(8):
                    dve.wait_ge(tp_ready, 8 * j + n + 1)
                    if n >= 2:
                        dve.wait_ge(u_ready, 8 * j + n - 1)
                    if A is None:
                        CP(buf[:, n % 2, :], PSA[:, 4 + n % 4, :]).then_inc(tp_val, 1)
                    else:
                        for kk in range(2):
                            k = 2 * n + kk
                            ins = TS(buf[:, n % 2, kk * TOK:(kk + 1) * TOK], PSA[:, 4 + n % 4, kk * TOK:(kk + 1) * TOK],
                                     A[:, k:k + 1], (Bc[:, k:k + 1] if Bc is not None else 0.0), ALU.mult, ALU.add)
                        ins.then_inc(tp_val, 1)
                    if n:
                        low(n - 1)
                low(7)

            def norm(j, s, src, A, Bc):
                variance(s)
                for t in range(TC):
                    TS(xn[:, t, :], src[:, t, :], stat[:, s, 2 + t:3 + t], None, ALU.mult).then_inc(xn_done, 1)
                transposes_lo(j, A, Bc)

            def modulated(n, scale, who, g):
                m = modT[:, scale * KD:(scale + 1) * KD, who]
                ch.link(STT(colA[:, n, :], m, 1.0, v_(g), ALU.add, ALU.mult))
                return colA[:, n, :]

            def shift(n, who):
                return modT[:, n * KD:(n + 1) * KD, who]

            def start():
                ch.link(dve.memset(cst[:, :, :].bitcast(F32), 0.0))
                dve.wait_ge(silu_done, 1)
                for w in range(2):
                    ch.link(CP(cst[:, :, 2 * w], csilu[:, w, :]))
                    ins = TT(cst[:, :, 2 * w + 1], csilu[:, w, :], cst[:, :, 2 * w], ALU.subtract)
                    if w == 0:
                        ch.link(ins)
                ins.then_inc(c_done, 1)
                norm(0, 0, h, v_("g_mix"), None)
                dve.wait_ge(ld["cb"], 48)
                ch.link(CP(levels[:, :], lev_in[:, :]))

            def mix1():
                dve.wait_ge(ld["cb"], 48)
                for s in range(NH + 3):
                    if s == 0:
                        ch.link(STT(bias[:, :], cB("dist"), -(2.0 ** (-8.0 / NH)), cB("logcount"), ALU.mult, ALU.add))
                    if s < NG:
                        dve.wait_ge(fa_ready, 2 * s + 2)
                        if s >= 2:
                            dve.wait_ge(fb_ready, s - 1)
                        CP(AB[:, s % 2, 1, :], PSA[:, 1, :]).then_inc(fa_dve, 1)
                    g = s - 2
                    if 0 <= g < NG:
                        dve.wait_ge(fc_hi, g + 1)
                        TT(ulo[:, 2 * g:2 * g + 2, :], PSA[:, 3, :], uhi[:, 2 * g:2 * g + 2, :], ALU.subtract).then_inc(fc_lo, 1)
                    hd = s - 1
                    if 0 <= hd < NH:
                        dve.wait_ge(sc_ready, hd + 1)
                        if hd >= 2:
                            dve.wait_ge(pt_ready, hd - 1)
                        L = lg[:, hd % 2, :, :]
                        ch.link(STT(L, PSA[:, 5, :], DH ** -0.5, bias[:, :], ALU.mult, ALU.add))
                        dve.tensor_reduce(astat[:, hd, 0:2], L, axis=AX.X, op=ALU.max, negate=True).then_inc(neg_max, 1)
                        if hd + 1 < NH:
                            ch.link(STT(bias[:, :], cB("dist"), -(2.0 ** (-8.0 * (hd + 2) / NH)), cB("logcount"), ALU.mult, ALU.add))
                        dve.wait_ge(exp_done, 2 * hd + 2)
                        ch.link(dve.reciprocal(astat[:, hd, 4:6], astat[:, hd, 2:4]))
                        for t in range(TC):
                            ins = TS(lg[:, hd % 2, t, :], lg[:, hd % 2, t, :], astat[:, hd, 4 + t:5 + t], None, ALU.mult)
                        ins.then_inc(prob_done, 1)
                    hd = s - 3
                    if 0 <= hd < NH:
                        dve.wait_ge(o_hi, hd + 1)
                        TT(ulo[:, 8 + hd, :], PSA[:, 7, 0:TOK], uhi[:, 8 + hd, :], ALU.subtract).then_inc(o_lo, 1)

            def final(s, after):
                variance(s)
                dve.wait_ge(ld["gf"], 16 if s == 2 else 32)
                for t in range(TC):
                    STT(h[:, t, :], h[:, t, :], stat[:, s, 2 + t:3 + t], gfin[:, :], ALU.mult, ALU.mult).then_inc(after, 1)

            def context():
                final(2, h_final)
                norm(2, 3, xc, modulated(2, 1, 1, "g_n1"), shift(0, 1))
                dve.wait_ge(B["ws_split"], 1)
                TT(wsl[:, :, :], wsr[:, :, :], wsh[:, :, :], ALU.subtract).then_inc(B["ws_low"], 1)

            LAf = LA[:, 2048:2064].rearrange("p (t z h) -> p t z h", t=TC, z=2)

            def gates(x):
                dve.wait_ge(B["nar_ready"], x + 1)
                CP(sm[:, :, :], PSA[:, 4, 0:64]).then_inc(B["nar_done"], 1)
                dve.wait_ge(B["nar_done"], x + 1)
                ch.link(dve.memset(gm[:, :, :, :, :], 0.0))
                for z in range(2):
                    c = 16 + 8 * z
                    TT(gm[:, :, z, 0, 4 * z:4 * z + 4], sm[:, :, c:c + 4], bgate[:, 8 * z:8 * z + 4].unsqueeze(1).broadcast_to([P, TC, 4]), ALU.add)
                    TT(LAf[:, :, z, :], sm[:, :, c + 4:c + 8], bgate[:, 8 * z + 4:8 * z + 8].unsqueeze(1).broadcast_to([P, TC, 4]), ALU.add)
                dve.wait_ge(ld["bl"], 16)
                dve.wait_ge(B["dec_ready"], x + 1)
                for t in range(TC):
                    ins = TT(LA[:, t * 1024:(t + 1) * 1024], PSA[:, 2 * t:2 * t + 2, :], blr[:, :, :], ALU.add)
                ins.then_inc(B["dec_done"], 1)
                dve.wait_ge(B["abs_done"], x + 1)
                STT(LA[:, :], LA[:, :], 0.0, TM[:, :], ALU.min, ALU.subtract).then_inc(B["gate_done"], 1)
                dve.wait_ge(B["gate_done"], x + 1)
                for z in range(2):
                    ins = CP(gm[:, :, z, 1, 4 * z:4 * z + 4], LAf[:, :, z, :])
                ins.then_inc(B["gm_done"], 1)

            def gate_rows_sum(x):
                dve.wait_ge(B["row_ready"], x + 1)
                CP(rows[:, 0:2, :], PSA[0:8, 6, :])
                ch.link(dve.memset(rows[:, 3, :], 0.0))
                ch.link(dve.tensor_tensor_scan(rows[:, 2, :], rows[:, 1, :], rows[:, 3, :], 0.0, ALU.add, ALU.add))

            def context_states():
                gates(0)
                for n in range(4):
                    z, t = n // 2, n % 2
                    dve.wait_ge(B["suf_exp"], n + 1)
                    TT(KE[:, n, :], KE[:, n, :], zc[:, t, 0, :], ALU.mult).then_inc(B["ke_done"], 1)
                gate_rows_sum(0)
                end = rows[:, 2, TOK - 1:TOK]
                ch.link(TS(rows[:, 4, :], rows[:, 2, :], -1.0, end, ALU.mult, ALU.add))
                ch.link(TT(rows[:, 4, :], rows[:, 4, :], rows[:, 0, :], ALU.add))
                ch.link(dve.tensor_reduce(mctx[:, 0:1], rows[:, 4, :], axis=AX.X, op=ALU.max))
                ch.link(TT(mctx[:, 0:1], mctx[:, 0:1], end, ALU.max))
                TS(mctx[:, 1:2], mctx[:, 0:1], -1.0, None, ALU.mult).then_inc(B["w_arg"], 1)
                dve.wait_ge(B["mr_exp"], 1)
                CP(rows[:, 6, :], rows[:, 5, ::-1]).then_inc(B["mr_rev"], 1)
                dve.wait_ge(B["wc_ready"], 1)
                ch.link(TS(wcol[:, :, :, :], PSA[:, 7, 0:32].rearrange("p (z t e) -> p z t e", z=2, t=TC), DK ** -0.5, None, ALU.mult))
                for n in range(4):
                    z, t = n // 2, n % 2
                    TT(WK[:, n, :].rearrange("p (e k) -> p e k", e=H), zc[:, t, 1, :].rearrange("p (e k) -> p e k", e=H),
                       wcol[:, z, t, 4 * z:4 * z + 4].unsqueeze(2).broadcast_to([P, H, DK]), ALU.mult).then_inc(B["wk_done"], 1)
                norm(3, 4, h, modulated(3, 1, 0, "g_n1"), shift(0, 0))

            def heads2():
                gates(1)
                dve.wait_ge(B["gqt_ready"], 2)
                CP(gkT[:, :, :], PSA[:, 2:4, :]).then_inc(B["gqt_dve"], 1)
                dve.wait_ge(B["dg_ready"], 1)
                two = cA("two_ident").unsqueeze(1).broadcast_to([P, 8, P])
                STf = ST[:, :, :, :].rearrange("p e t j -> p (e t) j")
                TT(STf, PSA[:, 4:6, :].rearrange("p b (c j) -> p (b c) j", j=P), two, ALU.mult).then_inc(B["dg_done"], 1)
                dve.wait_ge(B["dg_done"], 1)

                def take(m):
                    z, n = m // LEVELS, m % LEVELS
                    b0 = 2 if m % 2 else 6
                    dve.wait_ge(B["lv_ready"], m + 1)
                    if m:
                        dve.wait_ge(B["lv_done"], m)
                    mask = levels[:, m * P:(m + 1) * P].unsqueeze(1).broadcast_to([P, 8, P])
                    dve.copy_predicated(STf, mask, PSA[:, b0:b0 + 2, :].rearrange("p b (c j) -> p (b c) j", j=P)).then_inc(B["lv_done"], 1)

                for z in range(2):
                    dve.wait_ge(B["cum_done"], z + 1)
                    if z:
                        dve.wait_ge(B["eb_exp"], 1)
                    for n in range(LEVELS):
                        m = z * LEVELS + n
                        L = 2 ** n
                        if m:
                            dve.wait_ge(B["ke2_done"], m)
                            dve.wait_ge(B["qe_done"], m)
                        bv = bT[:, :, :].rearrange("p e (b l) -> p (e b) l", l=2 * L)
                        mid = L if z else L - 1
                        if z and n == 0:
                            dve.wait_ge(B["qb_done"], 1)
                        TT(EE[:, :, :].rearrange("p e (b l) -> p (e b) l", l=2 * L), bv,
                           bv[:, :, mid:mid + 1].broadcast_to([P, H * TOK // (2 * L), 2 * L]), ALU.subtract).then_inc(B["e_sub"], 1)
                        if m:
                            take(m - 1)
                        dve.wait_ge(B["e_exp"], m + 1)
                        TT(qE[:, :, :], gqT[:, :, :], EE[:, :, :], ALU.mult).then_inc(B["qe_done"], 1)
                    if z:
                        take(2 * LEVELS - 1)
                    dve.wait_ge(B["eb_exp"], z + 1)
                    TT(qB[:, z, :, :], gqT[:, :, :], EE[:, :, :], ALU.mult)
                    col = P if z else P - 1
                    CP(ebend[:, z, :], EE[:, :, col]).then_inc(B["qb_done"], 1)
                    dve.wait_ge(B["kt_exp"], z + 1)
                    TT(kte[:, :], kte[:, :], zl[:, z, 6, :], ALU.mult).then_inc(B["kt_done"], 1)
                    dve.wait_ge(B["s1_ready"], z + 1)
                    dve.wait_ge(B["qb_done"], z + 1)
                    for hd in range(H):
                        ins = STT(S1[z][:, hd, :], S0[:, z, hd, :], ebend[:, z, hd:hd + 1],
                                  PSA[:, hd // 2, (hd % 2) * DV:(hd % 2 + 1) * DV], ALU.mult, ALU.add)
                    ins.then_inc(B["s1_done"], 1)
                dve.wait_ge(B["mt_ready"], 2)
                TS(mkT[:, :, :], PSA[:, 2:4, :], DK ** -0.5, None, ALU.mult).then_inc(B["mt_dve"], 1)
                dve.wait_ge(B["go_done"], 4)
                gate_rows_sum(1)
                ch.link(TT(rows[:, 5, :], rows[:, 0, :], rows[:, 2, :], ALU.subtract))
                ch.link(dve.tensor_tensor_scan(rows[:, 4, :], rows[:, 5, :], rows[:, 5, :], mctx[:, 0:1], ALU.max, ALU.max))
                TS(rows[:, 9, :], rows[:, 4, :], -1.0, None, ALU.mult)
                TT(rows[:, 8, :], rows[:, 4, :], rows[:, 2, :], ALU.add).then_inc(B["w_arg"], 1)
                CP(rows[:, 6, :], rows[:, 5, ::-1])
                dve.wait_ge(B["mr_exp"], 2)
                CP(rows[:, 8, :], rows[:, 7, ::-1]).then_inc(B["mr_rev"], 1)
                dve.wait_ge(B["gc_ready"], 1)
                CP(gcol[:, :, :, :, :], PSA[:, 4, 0:64]).then_inc(B["gc_done"], 1)
                dve.wait_ge(B["gc_done"], 1)
                dve.wait_ge(ld["mm"], 16)

                def output(r):
                    z, hd = r // 4, r % 4
                    dve.wait_ge(B["mo_ready"], r + 1)
                    for jc in range(TC):
                        b_ = PSA[:, 4 + 2 * (r % 2) + jc, :]
                        ch.link(TS(hden[:, r % 2, jc, 2:3], b_[:, DV:DV + 1], -1.0, None, ALU.mult))
                        ch.link(TS(hden[:, r % 2, jc, 0:1], b_[:, DV:DV + 1], hden[:, r % 2, jc, 2:3], gcol[:, 1, z, jc, r:r + 1],
                                   ALU.max, ALU.max))
                    ch.link(dve.reciprocal(hden[:, r % 2, :, 1], hden[:, r % 2, :, 0]))
                    for jc in range(TC):
                        b_ = PSA[:, 4 + 2 * (r % 2) + jc, 0:DV]
                        dst = zl[:, jc, (1 if hd < 2 else 7), (hd % 2) * DV:(hd % 2 + 1) * DV]
                        if z == 0:
                            ins = TS(dst, b_, hden[:, r % 2, jc, 1:2], None, ALU.mult)
                        else:
                            ins = STT(dst, b_, hden[:, r % 2, jc, 1:2], dst, ALU.mult, ALU.add)
                    ins.then_inc(B["mo_done"], 1)

                for s in range(9):
                    if s < 8:
                        z, hd = s // 4, s % 4
                        dve.wait_ge(B["bc_ready"], s + 1)
                        if s >= 2:
                            dve.wait_ge(B["mo_ready"], s - 1)
                        for t in range(TC):
                            ins = STT(WW[:, s % 2, t, :], PSA[:, s % 2, 0:TOK], gcol[:, 0, z, t, s:s + 1], minmask[:, z, t, :], ALU.add, ALU.min)
                        ins.then_inc(B["w_dve"], 1)
                        if s == 0:
                            dve.wait_ge(B["mt_act"], 1)
                        TT(qI[:, s % 2, :], mqT[:, hd, :], PSA[:, s % 2, TOK:2 * TOK], ALU.mult).then_inc(B["qi_done"], 1)
                        dve.wait_ge(B["w_act"], s + 1)
                        dve.wait_ge(B["ms_ready"], s + 1)
                        TT(WW[:, s % 2, :, :], WW[:, s % 2, :, :], PSA[:, 2 + s % 2, :], ALU.mult).then_inc(B["sw_done"], 1)
                    if s >= 1:
                        if s - 1 == 4:
                            dve.wait_ge(B["mo_done"], 4)
                        output(s - 1)
                dve.wait_ge(B["ss_done"], 2 * 8)
                TS(rst[:, 0, :, :], rst[:, 0, :, :], 1.0 / DV, eps, ALU.mult, ALU.add).then_inc(B["rs_var"], 1)
                dve.wait_ge(B["rs_std"], 1)
                ch.link(dve.reciprocal(rst[:, 2, :, :], rst[:, 1, :, :]))
                dve.wait_ge(ld["gn"], 16)
                dve.wait_ge(B["silu_g"], 4)
                for t in range(TC):
                    for n in range(8):
                        o_ = zl[:, t, (0, 6, 1, 7)[n // 2], (n % 2) * DV:(n % 2 + 1) * DV]
                        ins = STT(o_, o_, rst[:, 2, t, n:n + 1], gnb[:, n // 4, :], ALU.mult, ALU.mult)
                    ch.link(ins)
                    for n in range(4):
                        g_ = zl[:, t, 2 + n, :]
                        ins = TT(g_, g_, zl[:, t, (0, 6, 1, 7)[n], :], ALU.mult)
                        if n % 2:
                            ins.then_inc(B["y_done"], 1)
                transposes_lo(4, None, None)
                gate_banks(0)

            def gate_banks(x):
                for n in range(4):
                    dve.wait_ge(B["gt_ready"], 4 * x + n + 1)
                    ins = CP(gtb[:, n * 512:(n + 1) * 512], PSA[:, n, :])
                ins.then_inc(B["gt_done"], 1)
                dve.wait_ge(B["gt_done"], x + 1)

            def out2():
                norm(5, 5, h, modulated(5, 4, 0, "g_n2"), shift(3, 0))
                gate_banks(1)

            interlude = {"in1": mix1, "out1": lambda: norm(1, 1, h, v_("g_mlp"), None), "dn1_3": context,
                         "inC": context_states, "inL": heads2, "out2": out2}
            flush = start
            before = None
            for p in PH:
                stream(p, flush, before if before is not None and before.mod and before.name != "in1" else None)
                before = p

                def flush(p=p):
                    evacuate(p, p.iters - 1, p.blocks - 1)
                    if p.name == "in1":
                        mod_add(7)
                    if p.name in interlude:
                        interlude[p.name]()
            flush()
            final(6, B["fin_done"])

        @block.gpsimd
        def _(pool):
            for m in range(2 * LEVELS):
                if m == 0:
                    pool.wait_ge(B["gqt_dve"], 1)
                else:
                    pool.wait_ge(B["lv_ready"], m)
                pool.wait_ge(B["e_exp"], m + 1)
                pool.tensor_tensor(kE[:, :, :], gkT[:, :, :], EE[:, :, :], ALU.mult).then_inc(B["ke2_done"], 1)


def constants():
    s = np.arange(P)
    t = np.arange(TOK)
    a = {"ident": np.eye(P), "flip": np.eye(P)[::-1], "suf": (s[:, None] > s[None, :]) / 16.0, "pre": (s[:, None] < s[None, :]) / 16.0,
         "inc_f": (s[:, None] <= s[None, :]) / 16.0, "inc_b": (s[:, None] >= s[None, :]) / 16.0, "one16": np.ones((P, P)) / 16.0,
         "ones": np.ones((P, P)), "two_ident": 2.0 * np.eye(P)}
    sel4 = np.zeros((P, 2))
    sel4[0:2, 0] = 1.0
    sel4[2:4, 1] = 1.0
    a["sel4"] = sel4
    const_a = np.concatenate([a[n] for n, _ in CONST_A], axis=1).astype(np.float32)

    ang = 2.0 * np.pi * ((t[:, None] * t[None, :]) % TOK) / TOK
    cos, sin = np.cos(ang) / 16.0, np.sin(ang) / 16.0
    chunks = lambda m: m.reshape(TC, P, -1).transpose(1, 0, 2).reshape(P, -1)
    d = np.abs(t[:, None] - t[None, :])
    count = (d <= 64).astype(int) + (d % 4 == 0) + (d % 16 == 0)
    logcount = np.where(count > 0, np.log(np.maximum(count, 1)), NEG)
    b = {"dft_pos": chunks(np.concatenate([cos, sin], axis=1)), "dft_cos": chunks(cos), "dft_nsin": chunks(-sin),
         "dist": chunks(d), "logcount": chunks(logcount)}
    const_b = np.concatenate([b[n] for n, _ in CONST_B], axis=1).astype(np.float32)

    i, j = s[:, None], s[None, :]
    lv = []
    for z in range(2):
        for n in range(LEVELS):
            L = 2 ** n
            same = (i // (2 * L)) == (j // (2 * L))
            first_i, first_j = (i % (2 * L)) < L, (j % (2 * L)) < L
            lv.append(same & first_i & ~first_j if z == 0 else same & ~first_i & first_j)
    levels = np.concatenate(lv, axis=1).astype(np.float32)

    key = s[:, None, None, None] + P * np.arange(TC)[None, None, :, None]
    qry = t[None, None, None, :]
    z = np.arange(2)[None, :, None, None]
    min_mask = np.where(np.where(z == 0, key <= qry, key >= qry), 0.0, NEG).astype(np.float32)
    return {"const_a": const_a, "const_b": const_b, "levels": levels, "min_mask": min_mask}


def token_tiles(w):
    k, n = w.shape
    return np.ascontiguousarray(w.reshape(k // 256, 2, P, n // NBLK, NBLK).transpose(3, 0, 2, 1, 4)).reshape(-1, P, TW)


def feature_tiles(w):
    k, n = w.shape
    return np.ascontiguousarray(w.reshape(2, 8, P, n // P, P).transpose(3, 0, 2, 1, 4)).reshape(-1, P, TW)


def columns(v):
    return np.asarray(v).reshape(-1, P).T


def layout(x, norm_mix_g, w_in, w_fourier, w_out, norm_mlp_g, w_up, w_down, norm_final_g, c_2, ctx_2, c_ctx_2, w_mod_2, b_mod_2,
           g_norm1_2, g_norm2_2, w_in_2, gla_w_lr_2, gla_b_lr_2, mlstm_b_gate_2, gla_g_norm_2, mlstm_g_norm_2, w_out_2, w_up_2,
           conv_w_2, conv_b_2, w_down_2, g_final_2):
    t = dict(constants())
    t["x"], t["ctx"] = np.asarray(x)[0], np.asarray(ctx_2)[0]
    t["w_in"] = token_tiles(np.asarray(w_in)[0])
    t["w_out"] = token_tiles(np.asarray(w_out)[0])
    t["w_up"] = feature_tiles(np.asarray(w_up)[0])
    t["w_down"] = np.concatenate([token_tiles(np.asarray(w_down)[0, q * 2048:(q + 1) * 2048]) for q in range(GROUPS1)])
    t["w_fourier"] = np.asarray(w_fourier)[0].reshape(NG, 2, P, 256).transpose(2, 0, 1, 3)
    t["w_mod"] = token_tiles(np.asarray(w_mod_2)[0])
    w = np.asarray(w_in_2)[0]
    at, part = 0, {}
    for name, n in (("gq", 512), ("gk", 512), ("gv", 1024), ("gg", 1024), ("lr", 16), ("mq", 512), ("mk", 512), ("mv", 1024),
                    ("mo", 1024), ("mg", 16)):
        part[name] = w[:, at:at + n]
        at += n
    t["w_in2"] = token_tiles(np.concatenate([part[n] for n in ("gq", "mq", "gg", "mo", "gk", "mk", "gv", "mv")], axis=1))
    t["w_in2_narrow"] = np.concatenate([part["lr"], part["mg"]], axis=1).reshape(KD, P, 32).transpose(1, 0, 2)
    t["w_lr"] = np.asarray(gla_w_lr_2)[0].transpose(1, 0, 2)
    t["b_lr"] = np.asarray(gla_b_lr_2)[0]
    t["b_gate"] = np.asarray(mlstm_b_gate_2)[0].reshape(16)
    t["g_heads"] = np.stack([np.asarray(gla_g_norm_2)[0], np.asarray(mlstm_g_norm_2)[0]])
    t["w_out2"] = token_tiles(np.asarray(w_out_2)[0])
    w = np.asarray(w_up_2)[0].reshape(D, 2, F2, P).transpose(0, 2, 1, 3).reshape(D, 2 * DFF2)
    t["w_up2"] = feature_tiles(w)
    w = np.asarray(w_down_2)[0]
    t["w_down2"] = np.concatenate([token_tiles(w[g * 2048:(g + 1) * 2048]) for g in range(2)])
    t["w_down2b"] = w[4096:].reshape(GROUP2[2], P, 4, NBLK).transpose(2, 1, 0, 3).reshape(4, P, GROUP2[2] * NBLK)
    t["g_final1"], t["g_final2"] = np.asarray(norm_final_g), np.asarray(g_final_2)
    conv = np.asarray(conv_w_2)[0].reshape(9, F2, P).transpose(2, 1, 0).reshape(P, F2 * 9)
    vec = {"g_mix": columns(norm_mix_g), "g_mlp": columns(norm_mlp_g), "g_n1": columns(g_norm1_2), "g_n2": columns(g_norm2_2),
           "c": columns(c_2), "cc": columns(c_ctx_2), "b_mod": columns(b_mod_2), "conv_w": conv, "conv_b": columns(conv_b_2)}
    t["vec"] = np.concatenate([vec[n] for n, _ in VEC], axis=1)
    return {n: np.ascontiguousarray(a) for n, a in t.items()}


def build(nc, arrays):
    t_in = {n: nc.dram_tensor("in_" + n, a.shape, mybir.dt.from_np(a.dtype), kind="ExternalInput").ap() for n, a in arrays.items()}
    out = nc.dram_tensor("out_0", (TOK, D), F32, kind="ExternalOutput").ap()
    program(nc, t_in, out)


def kernel(**inputs):
    import concourse.bacc as bacc
    from concourse.bass_utils import run_bass_kernel_spmd

    arrays = layout(**inputs)
    nc = bacc.Bacc("TRN2", target_bir_lowering=False, num_devices=1)
    build(nc, arrays)
    r = run_bass_kernel_spmd(nc, [{"in_" + n: a for n, a in arrays.items()}], core_ids=[0])
    return np.asarray(r.results[0]["out_0"]).reshape(1, TOK, D)
```

```python
import numpy as np
import concourse.bass as bass
from concourse import mybir
from contextlib import ExitStack

F32 = mybir.dt.float32
F32R = mybir.dt.float32r
U8 = mybir.dt.uint8
ALU = mybir.AluOpType
ACT = mybir.ActivationFunctionType
AX = mybir.AxisListType

P = 128
TOK = 256
TC = TOK // P
D = 2048
KD = D // P
EPS = 1e-6
NG = 4
NH = 8
DH = 128
DFF1 = 4 * D
H = 4
DK = 128
DV = 256
LR = 16
DFF2 = 5504
F2 = DFF2 // P
NMODCH = 6 * KD
LEVELS = 7
NEG = -1.0e30

SLOTS = 8
TW = 1024
LEAD = 4
NBLK = 512
GROUPS1 = 4
GROUP2 = (16, 16, 11)

CONST_A = [("ident", P), ("flip", P), ("suf", P), ("pre", P), ("inc_f", P), ("inc_b", P), ("one16", P),
           ("ones", P), ("two_ident", P), ("sel4", 2)]
CONST_B = [("dft_pos", 2 * 512), ("dft_cos", 2 * 256), ("dft_nsin", 2 * 256), ("dist", 512), ("logcount", 512)]


def offsets(spec):
    out, at = {}, 0
    for name, n in spec:
        out[name] = (at, n)
        at += n
    return out, at


OFF_A, NA = offsets(CONST_A)
OFF_B, NB_ = offsets(CONST_B)

VEC = [("g_mix", KD), ("g_mlp", KD), ("g_n1", KD), ("g_n2", KD), ("c", KD), ("cc", KD), ("b_mod", NMODCH),
       ("conv_w", F2 * 9), ("conv_b", F2)]
OFF_V, NV = offsets(VEC)


class Phase:

    def __init__(self, name, kind, iters, blocks, main, mod=0, k=None, evac=None, dest=0, mod0=0):
        self.name, self.kind, self.iters, self.blocks = name, kind, iters, blocks
        self.main, self.mod, self.k, self.evac, self.dest, self.mod0 = main, mod, k, evac, dest, mod0
        self.per_block = main + mod
        self.lead = LEAD
        self.per_iter = self.per_block * blocks
        self.order = [(kind, t) for t in range(main) for kind in (("mod", "main") if mod else ("main",))]


def plan():
    ph = [Phase("in1", "tok", 4, 2, 8, mod=8, k=KD, evac="z1", mod0=0),
          Phase("out1", "tok", 2, 2, 8, k=KD, evac="res")]
    for q in range(GROUPS1):
        ph.append(Phase(f"up1_{q}", "feat", 2, 2, 8, mod=8, evac="up1", mod0=8 + 4 * q))
        ph.append(Phase(f"dn1_{q}", "tok", 2, 2, 8, k=16, evac="res"))
    ph.append(Phase("inC", "tok", 3, 2, 8, k=KD, evac="zc", dest=6))
    ph.append(Phase("inL", "tok", 6, 2, 8, k=KD, evac="zl"))
    ph.append(Phase("out2", "tok", 2, 2, 8, k=KD, evac="gres"))
    for g, n in enumerate(GROUP2):
        if n % 4 == 0:
            ph.append(Phase(f"up2_{g}", "feat", n // 4, 2, 8, evac="up2", dest=0))
            ph.append(Phase(f"dn2_{g}", "tok", 2, 2, 8, k=n, evac="gres"))
        else:
            ph.append(Phase(f"up2_{g}", "feat", n // 4, 2, 8, evac="up2", dest=0))
            rest = n - 4 * (n // 4)
            if rest >= 2:
                ph.append(Phase(f"up2_{g}b", "feat", 1, 1, 8, evac="up2", dest=4 * (n // 4)))
            if rest % 2:
                ph.append(Phase(f"up2_{g}c", "feat", 1, 1, 4, evac="up2", dest=n - 1))
            ph.append(Phase(f"dn2_{g}", "tok", 1, 4, (n + 1) // 2, k=n, evac="gres"))
    seq = blk = 0
    for p in ph:
        if p.evac == "up2" and p.main == 8:
            p.lead = 5
        p.seq0, p.blk0 = seq, blk
        seq += p.per_iter * p.iters
        blk += p.blocks * p.iters
    return ph


class Chain:

    def __init__(self, eng, sem, base=0):
        self.eng, self.sem, self.base, self.k = eng, sem, base, 0

    def link(self, ins):
        self.k += 1
        ins.then_inc(self.sem, 1)
        self.eng.wait_ge(self.sem, self.base + self.k)


def turns(eng, n, body, after_first=None):
    body(0)
    if after_first is not None:
        after_first()
    if n > 1:
        with eng.Fori(1, n) as i:
            body(i)


def program(nc, t_in, out):
    PH = plan()
    BY = {p.name: p for p in PH}
    ctx = ExitStack()
    with ctx:
        cur = [16512]

        def at(name, shape, dt, offset=None):
            size = int(np.prod(shape[1:])) * (1 if dt == U8 else 4)
            if offset is None:
                offset = cur[0]
                cur[0] += (size + 63) // 64 * 64
                assert cur[0] <= 229344, (name, cur[0])
            return nc.alloc_sbuf_tensor_at(name, shape, dt, offset=offset)

        ring0 = cur[0]
        raw = at("raw", [P, SLOTS, TW], F32)
        wlo = at("wlo", [P, SLOTS, TW], F32R, ring0)
        whi = at("whi", [P, SLOTS, TW], F32R)
        u0 = cur[0]
        uhi = at("uhi", [P, KD, TOK], F32R)
        ulo = at("ulo", [P, KD, TOK], F32R)
        h = at("h", [P, TC, D], F32)
        ca = at("ca", [P, NA], F32)
        vec = at("vec", [P, NV], F32)
        modT = at("modT", [P, NMODCH, 2], F32)
        colA = at("colA", [P, 6, KD], F32)
        stat = at("stat", [P, 8, 4], F32)
        part = at("part", [P, TC, 4], F32)
        astat = at("astat", [P, NH, 8], F32)
        bgate = at("bgate", [P, 16], F32)
        levels = at("levels", [P, 2 * LEVELS * P], U8)
        Z = cur[0]
        K = 1024

        def z_at(name, shape, dt, off, in_u=False):
            size = int(np.prod(shape[1:])) * 4
            if in_u:
                assert off + size <= 32 * K
                return at(name, shape, dt, u0 + off)
            assert Z + off + size <= 229344, (name, Z + off + size - 229344)
            return at(name, shape, dt, Z + off)

        z1 = z_at("z1", [P, TC, 4096], F32, 0)
        cb = z_at("cb", [P, NB_], F32, 32 * K)
        wf = z_at("wf", [P, NG, 2, 256], F32, 44 * K)
        cst = z_at("cst", [P, KD, P], F32R, 52 * K)
        AB = z_at("AB", [P, 2, 2, 512], F32, 60 * K)
        lev_in = z_at("lev_in", [P, 2 * LEVELS * P], F32, 60 * K)
        re = z_at("re", [P, 2, TOK], F32, 68 * K)
        qk = z_at("qk", [P, 2, 512], F32, 70 * K)
        bias = z_at("bias", [P, 512], F32, 74 * K)
        lg = z_at("lg", [P, 2, TC, TOK], F32, 76 * K)
        pT = z_at("pT", [P, 2, 2, TOK], F32, 80 * K)
        xn = z_at("xn", [P, TC, D], F32, 0)
        tpv = z_at("tpv", [P, 2, 512], F32, 24 * K)
        tpy = z_at("tpy", [P, 2, 512], F32, 48 * K)
        ahi = z_at("ahi", [P, 16, TOK], F32R, 0)
        alo = z_at("alo", [P, 16, TOK], F32R, 16 * K)
        rl = z_at("rl", [P, 1024], F32, 68 * K)
        sq = z_at("sq", [P, 1024], F32, 72 * K)
        modrow = z_at("modrow", [P, 512], F32, 76 * K)
        csilu = z_at("csilu", [P, 2, KD], F32, 80 * K)
        gfin1 = z_at("gfin1", [P, D], F32, 52 * K)
        gfin = z_at("gfin", [P, D], F32, 40 * K)
        junk1 = z_at("junk1", [P, 512], F32, 68 * K)
        junk2 = z_at("junk2", [P, 512], F32, 80 * K)
        junk = z_at("junk", [P, D], F32, 68 * K)
        xc = z_at("xc", [P, TC, D], F32, 32 * K)
        zc = z_at("zc", [P, TC, 6, 512], F32, 0)
        zl = z_at("zl", [P, TC, 12, 512], F32, 0)
        LA = z_at("LA", [P, 2064], F32, 48 * K)
        WK = z_at("WK", [P, 4, 512], F32, 24 * K)
        KE = z_at("KE", [P, 4, 512], F32, 32 * K)
        S0 = z_at("S0", [P, 2, H, DV], F32, 57 * K)
        CN = z_at("CN", [P, 2, H, 258], F32, 65 * K)
        wsr = z_at("wsr", [P, KD, 32], F32, 60 * K)
        wsh = z_at("wsh", [P, KD, 32], F32R, 74 * K)
        wsl = z_at("wsl", [P, KD, 32], F32R, 76 * K)
        blr = z_at("blr", [P, 2, 512], F32, 78 * K)
        TM = z_at("TM", [P, 2064], F32, 30 * K)
        glrT = z_at("glrT", [32, TOK], F32, 39 * K)
        wlr = z_at("wlr", [LR, 2, 512], F32, 40 * K)
        qB = z_at("qB", [P, 2, H, TOK], F32, 74 * K)
        gtb = z_at("gtb", [P, D], F32, 74 * K)
        small = 82 * K
        sm = z_at("sm", [P, TC, 32], F32, small)
        gm = z_at("gm", [P, TC, 2, 2, 8], F32, small + 256)
        wcol = z_at("wcol", [P, 2, TC, 8], F32, small + 512)
        ebend = z_at("ebend", [P, 2, H], F32, small + 640)
        mctx = z_at("mctx", [8, 4], F32, small + 704)
        kte = z_at("kte", [P, 512], F32, small + 768)
        gcol = z_at("gcol", [P, 2, 2, TC, 8], F32, small + 768)
        hden = z_at("hden", [P, 2, TC, 4], F32, small + 1024 + 256)
        rst = z_at("rst", [P, 4, TC, 8], F32, small + 1024 + 512)
        bT = z_at("bT", [P, H, TOK], F32, 0, True)
        EE = z_at("EE", [P, H, TOK], F32, 4 * K, True)
        gqT = z_at("gqT", [P, H, TOK], F32, 8 * K, True)
        gkT = z_at("gkT", [P, H, TOK], F32, 12 * K, True)
        EE2 = z_at("EE2", [P, H, TOK], F32, 78 * K)
        EEs = [EE, EE2]
        qE = z_at("qE", [P, H, TOK], F32, 16 * K, True)
        kE = z_at("kE", [P, H, TOK], F32, 20 * K, True)
        ST = z_at("ST", [P, H, TC, P], F32, 24 * K, True)
        S1 = [z_at("S1a", [P, H, DV], F32, 28 * K, True), z_at("S1b", [P, H, DV], F32, 16 * K, True)]
        mqT = z_at("mqT", [P, H, TOK], F32, 0, True)
        mkT = z_at("mkT", [P, H, TOK], F32, 4 * K, True)
        WW = z_at("WW", [P, 2, TC, TOK], F32, 8 * K, True)
        qI = z_at("qI", [P, 2, TOK], F32, 12 * K, True)
        minmask = z_at("minmask", [P, 2, TC, TOK], F32, 14 * K, True)
        gnb = z_at("gnb", [P, 2, DV], F32, 18 * K, True)
        rows = z_at("rows", [8, 11, TOK], F32, 20 * K, True)
        sqj = z_at("sqj", [P, TC, 8, DV], F32, 57 * K)
        cv = z_at("cv", [P, 2, TOK], F32, 48 * K)
        sl = z_at("sl", [P, 2, TOK], F32, 50 * K)
        sv = z_at("sv", [P, 2, TOK], F32, 52 * K)
        gtmp = z_at("gtmp", [P, TC, 512], F32, 56 * K)
        PSA = ctx.enter_context(nc.psum_tensor("PSA", [P, 8, 512], F32))
        acc = PSA[:, 0:4, :]

        sem_names = {}

        def sem(name):
            sem_names[name] = ctx.enter_context(nc.semaphore(name))
            return sem_names[name]

        arrived = [sem(f"arrived{n}") for n in range(SLOTS)]
        hi_done, lo_done, tile_used = sem("hi_done"), sem("lo_done"), sem("tile_used")
        acc_free = sem("acc_free")
        row_done, mini_ready, mini_done = (sem(n) for n in ("row_done", "mini_ready", "mini_done"))
        u_ready = sem("u_ready")
        a_ready = sem("a_ready")
        ld = {n: sem("ld_" + n) for n in ("x", "const", "vec", "cb", "lev", "wf", "xc", "ws", "wlr", "gf", "bl", "mm", "gn", "out")}
        act_step, dve_step, evac_step = sem("act_step"), sem("dve_step"), sem("evac_step")
        c_done, silu_done = sem("c_done"), sem("silu_done")
        sq_part = sem("sq_part")
        sumsq, varr, stdd, xn_done, tp_ready, tp_val, tp_hi = (sem(n) for n in (
            "sumsq", "varr", "stdd", "xn_done", "tp_ready", "tp_val", "tp_hi"))
        fa_ready, fa_act, fa_dve, fb_ready, fb_done, fc_ready, fc_hi, fc_lo = (sem(n) for n in (
            "fa_ready", "fa_act", "fa_dve", "fb_ready", "fb_done", "fc_ready", "fc_hi", "fc_lo"))
        qk_ready, qk_done, sc_ready, neg_max, exp_done, prob_done, pt_ready, pt_done, o_ready, o_hi, o_lo = (sem(n) for n in (
            "qk_ready", "qk_done", "sc_ready", "neg_max", "exp_done", "prob_done", "pt_ready", "pt_done", "o_ready", "o_hi", "o_lo"))
        h_final = sem("h_final")
        act_sq, a_hi, cv_done, sl_done = (sem(n) for n in ("act_sq", "a_hi", "cv_done", "sl_done"))
        blk2 = {n: sem(n) for n in (
            "ws_split", "nar_ready", "nar_done", "col_ready", "mulcol", "glr_ready", "glr_done", "dec_ready", "dec_done",
            "abs_done", "gate_done", "gm_done", "row_ready", "row_copy", "suf_ready", "suf_exp", "ke_done", "st_ready",
            "st_done", "w_arg", "w_exp", "wc_ready", "wk_done", "cn_ready", "cn_done", "gqt_ready", "gqt_act",
            "gqt_dve", "dg_ready", "dg_done", "cum_ready", "cum_done", "e_sub", "e_exp", "qe_done", "ke2_done", "lv_ready",
            "lv_done", "eb_exp", "qb_done", "kt_ready", "kt_exp", "kt_done", "s1_ready", "s1_done", "go_ready", "go_done",
            "mt_ready", "mt_act", "mt_dve", "mr_dve", "mr_exp", "mr_rev", "gc_ready", "gc_done", "bc_ready", "w_dve",
            "w_act", "qi_done", "ms_ready", "sw_done", "mo_ready", "mo_done", "ss_done", "rs_var", "rs_std", "silu_g", "ws_low",
            "y_done", "gt_ready", "gt_done", "fin_done", "zero_done", "diag_free")}
        B = blk2

        ident = ca[:, OFF_A["ident"][0]:OFF_A["ident"][0] + P]

        def cA(name):
            a, n = OFF_A[name]
            return ca[:, a:a + n]

        def cB(name):
            a, n = OFF_B[name]
            return cb[:, a:a + n]

        def v_(name):
            a, n = OFF_V[name]
            return vec[:, a:a + n]

        eps = EPS
        NORMS = ["mix", "mlp", "ctx", "lat", "y2", "n2"]
        OUTU = {"mix": "in1", "mlp": "up1_0", "ctx": "inC", "lat": "inL", "n2": "up2_0"}

        SUMMED = {"out1": 1, "dn1_3": 3, "out2": 5, "dn2_2": 6}
        NARROW = {"inC": 0, "inL": 1}

        STEPS = {"gres": 1, "up2": 8}
        E0, at_ = {}, 0
        for p in PH:
            E0[p.name] = at_
            at_ += STEPS.get(p.evac, 0) * p.iters * p.blocks
        A0, at_ = {}, 0
        for p in PH:
            if p.evac == "up2":
                A0[p.name] = at_
                at_ += p.iters * p.blocks

        block = ctx.enter_context(nc.Block())

        @block.sync
        def _(sp):
            def load(dst, src, name):
                sp.dma_start(dst, src).then_inc(ld[name], 16)

            def tile(src, p, i, t):
                n = p.seq0 % SLOTS + t
                if isinstance(i, int) and p.seq0 + p.per_iter * i + t < SLOTS:
                    pass
                else:
                    sp.wait_ge(tile_used, p.seq0 + t + 1 - SLOTS + i * p.per_iter)
                w = src.shape[-1]
                sp.dma_start(raw[:, n % SLOTS, 0:w], src).then_inc(arrived[n % SLOTS], 16)

            def stream(p):
                def body(i):
                    for b in range(p.blocks):
                        for at, (kind, t) in enumerate(p.order):
                            n = (i * p.blocks + b)
                            if kind == "mod":
                                src = t_in["w_mod"][(n + p.mod0) * 8 + t]
                            elif p.evac == "z1":
                                src = t_in["w_in"][n * 8 + t]
                            elif p.name == "out1":
                                src = t_in["w_out"][n * 8 + t]
                            elif p.name == "out2":
                                src = t_in["w_out2"][n * 8 + t]
                            elif p.evac == "up1":
                                src = t_in["w_up"][int(p.name[4:]) * 32 + n * 8 + t]
                            elif p.name.startswith("dn1"):
                                src = t_in["w_down"][int(p.name[4:]) * 32 + n * 8 + t]
                            elif p.evac == "zc":
                                src = t_in["w_in2"][(n + 6) * 8 + t]
                            elif p.evac == "zl":
                                src = t_in["w_in2"][n * 8 + t]
                            elif p.evac == "up2":
                                g = int(p.name[4])
                                src = t_in["w_up2"][(g * 16 + p.dest) * 4 + n * 8 + t]
                            elif p.k == 16:
                                src = t_in["w_down2"][int(p.name[4]) * 32 + n * 8 + t]
                            else:
                                w = min(TW, p.k * NBLK - t * TW)
                                src = t_in["w_down2b"][n, :, t * TW:t * TW + w]
                            tile(src, p, i, b * p.per_block + at)
                            if isinstance(i, int) and i == 0 and b == 0 and at == p.lead - 1:
                                extra(p)
                turns(sp, p.iters, body)

            load(vec[:, :], t_in["vec"], "vec")
            for t in range(TC):
                load(h[:, t, :], t_in["x"][t * P:(t + 1) * P, :], "x")
            load(ca[:, :], t_in["const_a"], "const")

            def extra(p):
                if p.name == "in1":
                    load(lev_in[:, :], t_in["levels"], "lev")
                    load(bgate[:, :], t_in["b_gate"].partition_broadcast(P), "cb")
                    load(cb[:, :], t_in["const_b"], "cb")
                    load(wf[:, :, :, :], t_in["w_fourier"], "wf")
                if p.name == "dn1_3":
                    for t in range(TC):
                        load(xc[:, t, :], t_in["ctx"][t * P:(t + 1) * P, :], "xc")
                    sp.wait_ge(tile_used, p.seq0)
                    load(gfin1[:, :], t_in["g_final1"].partition_broadcast(P), "gf")
                if p.name == "inC":
                    sp.wait_ge(h_final, 2)
                    load(wsr[:, :, :], t_in["w_in2_narrow"], "ws")
                    load(blr[:, :, :], t_in["b_lr"].partition_broadcast(P), "bl")
                    sp.wait_ge(tp_ready, 24)
                    load(wlr[:, :, :], t_in["w_lr"], "wlr")
                if p.name == "out2":
                    sp.wait_ge(tile_used, BY["out2"].seq0)
                    sp.wait_ge(B["go_done"], 4)
                    load(minmask[:, :, :, :], t_in["min_mask"], "mm")
                    load(gnb[:, :, :], t_in["g_heads"].partition_broadcast(P), "gn")
                if p.name == "up2_1":
                    load(gfin[:, :], t_in["g_final2"].partition_broadcast(P), "gf")

            for p in PH:
                stream(p)
            for t in range(TC):
                sp.wait_ge(B["fin_done"], t + 1)
                sp.dma_start(out[t * P:(t + 1) * P, :], h[:, t, :]).then_inc(ld["out"], 16)
            sp.wait_ge(ld["out"], 16 * TC)

        @block.tensor
        def _(pe):
            def weights(p, i, t):
                pe.wait_ge(lo_done, p.seq0 + t + 1 + i * p.per_iter)
                n = (p.seq0 + t) % SLOTS
                return whi[:, n, :], wlo[:, n, :]

            def product(dst, xh, xl, wh, wl, start, stop):
                pe.matmul(dst, xh, wh, start=start, stop=False)
                pe.matmul(dst, xh, wl, start=False, stop=False)
                return pe.matmul(dst, xl, wh, start=False, stop=stop)

            def mod_columns(mb):
                pe.wait_ge(row_done, mb + 1)
                if not (isinstance(mb, int) and mb == 0):
                    pe.wait_ge(mini_done, mb)
                for c in range(4):
                    mm = pe.matmul(PSA[:, 5, 2 * c:2 * c + 2], modrow[0:4, c * P:(c + 1) * P], cA("sel4")[0:4, 0:2], start=True, stop=True)
                mm.then_inc(mini_ready, 1)

            def narrow(x, part):
                if part == 0:
                    pe.wait_ge(B["ws_low"], 1)
                    pe.wait_ge(u_ready, 24 + 8 * x)
                    for k in range(KD):
                        mm = product(PSA[0:32, 4, 0:TOK], wsh[:, k, :], wsl[:, k, :], uhi[:, k, :], ulo[:, k, :], k == 0, k == KD - 1)
                    mm.then_inc(B["nar_ready"], 1)
                elif part == 1:
                    pe.wait_ge(B["glr_done"], x + 1)
                    for t in range(TC):
                        mm = pe.transpose(PSA[:, 5, t * 32:(t + 1) * 32], glrT[:, t * P:(t + 1) * P], ident[0:32, 0:32])
                    mm.then_inc(B["glr_ready"], 1)
                else:
                    pe.wait_ge(B["nar_done"], x + 1)
                    pe.wait_ge(ld["wlr"], 16)
                    for t in range(TC):
                        for z in range(2):
                            mm = pe.matmul(PSA[:, 4 + 2 * t + z, :], glrT[0:LR, t * P:(t + 1) * P], wlr[:, z, :], start=True, stop=True)
                    mm.then_inc(B["dec_ready"], 1)

            def narrow_parts(x):
                return {(0, 4): lambda: narrow(x, 0), (0, 6): lambda: narrow(x, 1), (1, 1): lambda: narrow(x, 2)}

            def stream(p, u0=None, a0=None, before=None, between={}):
                def body(i):
                    first = isinstance(i, int) and i == 0
                    for b in range(p.blocks):
                        nblk = p.blk0 + b + i * p.blocks
                        buf = b % 2 if p.blocks % 2 == 0 else p.blk0 % 2
                        new = first and b == 0
                        for at, (kind, t) in enumerate(p.order):
                            if kind == "mod":
                                mb = p.mod0 + b + i * p.blocks
                                if t == 0 and not (isinstance(mb, int) and mb < 2):
                                    pe.wait_ge(row_done, mb - 1)
                                wh, wl = weights(p, i, b * p.per_block + at)
                                for kk in range(2):
                                    k = 2 * t + kk
                                    lhs = cst[:, k, :]
                                    pe.matmul(PSA[:, 4 + 2 * (b % 2), :], lhs, wh[:, kk * 512:kk * 512 + 512], start=k == 0, stop=False)
                                    mm = pe.matmul(PSA[:, 4 + 2 * (b % 2), :], lhs, wl[:, kk * 512:kk * 512 + 512], start=False, stop=k == KD - 1)
                                mm.then_inc(tile_used, 1)
                            else:
                                if t == 0 and not (isinstance(nblk, int) and nblk < 2):
                                    pe.wait_ge(acc_free, nblk - 1)
                                if new and u0 is not None:
                                    if p.kind == "tok":
                                        pe.wait_ge(u_ready, u0 + t + 1)
                                    elif t < 2:
                                        pe.wait_ge(u_ready, u0 + 4 * t + 4)
                                if new and a0 is not None:
                                    per = 4 if p.name.startswith("dn1") else 2
                                    pe.wait_ge(a_ready, a0 + (min(2 * t + 2, p.k) + per - 1) // per)
                                wh, wl = weights(p, i, b * p.per_block + at)
                                if p.kind == "tok":
                                    xh, xl = (ahi, alo) if p.name.startswith("dn") else (uhi, ulo)
                                    for kk in range(2):
                                        k = 2 * t + kk
                                        if k >= p.k:
                                            continue
                                        for tt in range(TC):
                                            c = slice(kk * 512, kk * 512 + 512)
                                            s_ = slice(tt * P, (tt + 1) * P)
                                            mm = product(acc[:, 2 * buf + tt, :], xh[:, k, s_], xl[:, k, s_], wh[:, c], wl[:, c], k == 0, k == p.k - 1)
                                else:
                                    f, half = t // 2, t % 2
                                    dst = acc[:, 2 * buf + f // 2, (f % 2) * TOK:(f % 2 + 1) * TOK]
                                    for kk in range(8):
                                        k = 8 * half + kk
                                        c = slice(kk * P, (kk + 1) * P)
                                        mm = product(dst, wh[:, c], wl[:, c], uhi[:, k, :], ulo[:, k, :], k == 0, k == KD - 1)
                                mm.then_inc(tile_used, 1)
                            if first and (b, at) in between:
                                between[b, at]()
                            if at == 3:
                                if p.mod and not new:
                                    mod_columns(p.mod0 + b - 1 + i * p.blocks)
                                if new and before is not None:
                                    mod_columns(before.mod0 + before.iters * before.blocks - 1)
                turns(pe, p.iters, body)

            def transposes(j, ns):
                banks = (4, 5, 6, 7) if j == 2 else (2, 3, 5, 7)
                for n in ns:
                    if n == 0 and j != 4:
                        pe.wait_ge(xn_done, 2 * [0, 1, 2, 3, None, 4][j] + 2)
                    elif n == 0:
                        pe.wait_ge(B["y_done"], 4)
                    if n >= 4:
                        pe.wait_ge(tp_val, 8 * j + n - 3)
                    for kk in range(2):
                        for t in range(TC):
                            k = 2 * n + kk
                            if j == 4:
                                src = zl[:, t, 2 + k // 4, (k % 4) * P:(k % 4 + 1) * P]
                            elif j == 2:
                                src = xc[:, t, k * P:(k + 1) * P]
                            else:
                                src = xn[:, t, k * P:(k + 1) * P]
                            mm = pe.transpose(PSA[:, banks[n % 4], kk * TOK + t * P:kk * TOK + (t + 1) * P], src, ident)
                    mm.then_inc(tp_ready, 1)

            def rest_of_transposes(p, j):
                main = [at for at, (kind, _) in enumerate(p.order) if kind == "main"]
                ready = [at for at in main if at < p.lead]
                ns = [[4 + n] for n in range(len(ready) - 1)] + [list(range(3 + len(ready), 8))]
                return {(0, at): lambda n=n: transposes(j, n) for at, n in zip(ready, ns)}

            def gate_rows(first):
                for n in range(4):
                    for c in range(4):
                        mm = pe.matmul(PSA[:, n, c * P:(c + 1) * P], modT[:, first + 4 * n + c, 0:1].broadcast_to([P, P]), ident,
                                       start=True, stop=True)
                    mm.then_inc(B["gt_ready"], 1)

            pe.wait_ge(ld["const"], 16)
            transposes(0, range(4))
            pe.wait_ge(c_done, 1)
            stream(BY["in1"], u0=0, between=rest_of_transposes(BY["in1"], 0))
            mod_columns(7)

            pe.wait_ge(ld["cb"], 32)
            pe.wait_ge(ld["wf"], 16)
            pe.wait_ge(acc_free, BY["out1"].blk0)
            pe.wait_ge(mini_done, 8)
            for s in range(NH + 3):
                if s < NG:
                    if s >= 1:
                        pe.wait_ge(fa_act, s)
                        pe.wait_ge(fa_dve, s)
                    for c in range(2):
                        for t in range(TC):
                            mm = pe.matmul(PSA[:, c, :], z1[:, t, s * 256 + c * P:s * 256 + (c + 1) * P],
                                           cB("dft_pos")[:, t * 512:(t + 1) * 512], start=t == 0, stop=t == 1)
                        mm.then_inc(fa_ready, 1)
                g = s - 1
                if 0 <= g < NG:
                    pe.wait_ge(fa_act, g + 1)
                    pe.wait_ge(fa_dve, g + 1)
                    if g >= 1:
                        pe.wait_ge(fb_done, g)
                    for c2 in range(2):
                        for c in range(2):
                            for m, (name, part) in enumerate((("dft_cos", 0), ("dft_nsin", 1))):
                                mm = pe.matmul(PSA[:, 2, c2 * TOK:(c2 + 1) * TOK], cB(name)[:, c * 256 + c2 * P:c * 256 + (c2 + 1) * P],
                                               AB[:, g % 2, c, part * TOK:(part + 1) * TOK], start=c == 0 and m == 0, stop=c == 1 and m == 1)
                    mm.then_inc(fb_ready, 1)
                g = s - 2
                if 0 <= g < NG:
                    pe.wait_ge(fb_done, g + 1)
                    if g >= 1:
                        pe.wait_ge(fc_hi, g)
                        pe.wait_ge(fc_lo, g)
                    for e in range(2):
                        for c in range(2):
                            mm = pe.matmul(PSA[:, 3, e * TOK:(e + 1) * TOK], wf[:, g, c, e * P:(e + 1) * P], re[:, c, :],
                                           start=c == 0, stop=c == 1)
                    mm.then_inc(fc_ready, 1)
                if s < NH:
                    if s >= 1:
                        pe.wait_ge(qk_done, s)
                    for n, c0 in enumerate((1024, 2048)):
                        for t in range(TC):
                            mm = pe.transpose(PSA[:, 4, n * TOK + t * P:n * TOK + (t + 1) * P], z1[:, t, c0 + s * DH:c0 + (s + 1) * DH], ident)
                    mm.then_inc(qk_ready, 1)
                hd = s - 1
                if 0 <= hd < NH:
                    pe.wait_ge(qk_done, hd + 1)
                    if hd >= 1:
                        pe.wait_ge(neg_max, hd)
                    for t in range(TC):
                        mm = pe.matmul(PSA[:, 5, t * TOK:(t + 1) * TOK], qk[:, hd % 2, t * P:(t + 1) * P], qk[:, hd % 2, TOK:2 * TOK],
                                       start=True, stop=True)
                    mm.then_inc(sc_ready, 1)
                hd = s - 2
                if 0 <= hd < NH:
                    pe.wait_ge(prob_done, hd + 1)
                    if hd >= 1:
                        pe.wait_ge(pt_done, hd)
                    for kc in range(TC):
                        for t in range(TC):
                            mm = pe.transpose(PSA[:, 6, kc * TOK + t * P:kc * TOK + (t + 1) * P], lg[:, hd % 2, t, kc * P:(kc + 1) * P], ident)
                    mm.then_inc(pt_ready, 1)
                hd = s - 3
                if 0 <= hd < NH:
                    pe.wait_ge(pt_done, hd + 1)
                    if hd >= 1:
                        pe.wait_ge(o_hi, hd)
                        pe.wait_ge(o_lo, hd)
                    for kc in range(TC):
                        mm = pe.matmul(PSA[:, 7, 0:TOK], z1[:, kc, 3072 + hd * DH:3072 + (hd + 1) * DH], pT[:, hd % 2, kc, :],
                                       start=kc == 0, stop=kc == 1)
                    mm.then_inc(o_ready, 1)
            pe.wait_ge(fc_lo, NG)
            pe.wait_ge(o_lo, NH)
            stream(BY["out1"])
            transposes(1, range(8))
            for q in range(GROUPS1):
                stream(BY[f"up1_{q}"], u0=8 if q == 0 else None)
                stream(BY[f"dn1_{q}"], a0=4 * q, before=BY[f"up1_{q}"], between={} if q < GROUPS1 - 1 else {
                    (1, 2): lambda: transposes(2, range(4)), (1, 3): lambda: transposes(2, (4, 5)),
                    (1, 4): lambda: transposes(2, (6, 7))})
            stream(BY["inC"], u0=16, between=narrow_parts(0))

            def gate_matrix_rows(x):
                pe.wait_ge(B["gm_done"], x + 1)
                for kind in range(2):
                    for t in range(TC):
                        dst = PSA[0:8, 6, kind * TOK + t * P:kind * TOK + (t + 1) * P]
                        pe.matmul(dst, gm[:, t, 0, kind, :], ident, start=True, stop=False)
                        mm = pe.matmul(dst, gm[:, 1 - t, 1, kind, :], cA("flip"), start=False, stop=True)
                mm.then_inc(B["row_ready"], 1)

            def LA4(t, z):
                return LA[:, (2 * t + z) * 512:(2 * t + z + 1) * 512]

            gate_matrix_rows(0)
            pe.wait_ge(acc_free, BY["inL"].blk0)
            for z in range(2):
                for t in range(TC):
                    dst = PSA[:, 2 * z + t, :]
                    if z == 0 and t == 0:
                        pe.matmul(dst, cA("suf"), LA4(0, 0), start=True, stop=False)
                        mm = pe.matmul(dst, cA("one16"), LA4(1, 0), start=False, stop=True)
                    elif z == 0:
                        mm = pe.matmul(dst, cA("suf"), LA4(1, 0), start=True, stop=True)
                    elif t == 0:
                        mm = pe.matmul(dst, cA("pre"), LA4(0, 1), start=True, stop=True)
                    else:
                        pe.matmul(dst, cA("one16"), LA4(0, 1), start=True, stop=False)
                        mm = pe.matmul(dst, cA("pre"), LA4(1, 1), start=False, stop=True)
            mm.then_inc(B["suf_ready"], 1)
            pe.wait_ge(B["mr_rev"], 1)
            for z in range(2):
                for t in range(TC):
                    mm = pe.transpose(PSA[:, 7, (2 * z + t) * 8:(2 * z + t + 1) * 8], rows[:, 5 + z, t * P:(t + 1) * P], ident[0:8, 0:8])
            mm.then_inc(B["wc_ready"], 1)
            pe.wait_ge(B["ke_done"], 4)
            for z in range(2):
                for h2 in range(2):
                    for hh in range(2):
                        hd = 2 * h2 + hh
                        for t in range(TC):
                            mm = pe.matmul(PSA[:, 2 * z + h2, hh * DV:(hh + 1) * DV], KE[:, 2 * z + t, hd * DK:(hd + 1) * DK],
                                           zc[:, t, 2 + h2, hh * DV:(hh + 1) * DV], start=t == 0, stop=t == 1)
                    mm.then_inc(B["st_ready"], 1)
            pe.wait_ge(B["wk_done"], 4)
            for n in range(8):
                z, hd = n // 4, n % 4
                if n >= 2:
                    pe.wait_ge(B["cn_done"], n - 1)
                for t in range(TC):
                    pe.matmul(PSA[:, 4 + n % 2, 0:DV], WK[:, 2 * z + t, hd * DK:(hd + 1) * DK],
                              zc[:, t, 4 + hd // 2, (hd % 2) * DV:(hd % 2 + 1) * DV], start=t == 0, stop=t == 1)
                for t in range(TC):
                    mm = pe.matmul(PSA[:, 4 + n % 2, DV:DV + 2], WK[:, 2 * z + t, hd * DK:(hd + 1) * DK], cA("ones")[:, 0:2],
                                   start=t == 0, stop=t == 1)
                mm.then_inc(B["cn_ready"], 1)
            pe.wait_ge(B["cn_done"], 8)
            pe.wait_ge(B["st_done"], 4)

            transposes(3, range(4))
            stream(BY["inL"], u0=24, between={**rest_of_transposes(BY["inL"], 3), **narrow_parts(1)})

            def running_decay(z, b0):
                for hd in range(H):
                    for t in range(TC):
                        mm = pe.matmul(PSA[:, b0 + hd // 2, (hd % 2) * TOK + t * P:(hd % 2) * TOK + (t + 1) * P],
                                       LA4(t, z)[:, hd * DK:(hd + 1) * DK], cA("inc_b" if z else "inc_f"), start=True, stop=True)
                mm.then_inc(B["cum_ready"], 1)

            pe.wait_ge(B["gm_done"], 2)
            running_decay(0, 6)
            pe.wait_ge(acc_free, BY["out2"].blk0)
            for n, blk in enumerate((0, 6)):
                for hd in range(H):
                    for t in range(TC):
                        mm = pe.transpose(PSA[:, 2 * n + hd // 2, (hd % 2) * TOK + t * P:(hd % 2) * TOK + (t + 1) * P],
                                          zl[:, t, blk, hd * DK:(hd + 1) * DK], ident)
                mm.then_inc(B["gqt_ready"], 1)

            def keys(m, hd, s_):
                return kE[:, hd, s_] if m % 2 == 0 else zl[:, hd // 2, 0, (hd % 2) * TOK + s_.start:(hd % 2) * TOK + s_.stop]

            def scores(lq, lk, b0):
                for hd in range(H):
                    for t in range(TC):
                        c = hd * TC + t
                        mm = pe.matmul(PSA[:, b0 + c // 4, (c % 4) * P:(c % 4 + 1) * P], lk(hd, slice(t * P, (t + 1) * P)),
                                       lq[:, hd, t * P:(t + 1) * P], start=True, stop=True)
                return mm

            pe.wait_ge(B["gqt_act"], 1)
            pe.wait_ge(B["gqt_dve"], 1)
            scores(gqT, lambda hd, s_: gkT[:, hd, s_], 4).then_inc(B["dg_ready"], 1)
            for z in range(2):
                if z:
                    pe.wait_ge(B["cum_done"], 1)
                    running_decay(1, 0)
                for n in range(LEVELS):
                    m = z * LEVELS + n
                    pe.wait_ge(B["qe_done"], m + 1)
                    pe.wait_ge(B["ke2_done"], m + 1)
                    if m >= 2:
                        pe.wait_ge(B["lv_done"], m - 1)
                    scores(qE, lambda hd, s_, m=m: keys(m, hd, s_), 2 if m % 2 else 6).then_inc(B["lv_ready"], 1)
                pe.wait_ge(B["dg_done"], 1)
                if z:
                    pe.wait_ge(B["s1_done"], 1)
                pe.matmul(PSA[:, 4, :], cA("pre" if z else "suf"), LA4(z, z), start=True, stop=True).then_inc(B["kt_ready"], 1)
                pe.wait_ge(B["kt_done"], z + 1)
                pe.wait_ge(B["cum_done"], z + 1)
                for hd in range(H):
                    mm = pe.matmul(PSA[:, hd // 2, (hd % 2) * DV:(hd % 2 + 1) * DV], kte[:, hd * DK:(hd + 1) * DK],
                                   zl[:, z, 8 + hd // 2, (hd % 2) * DV:(hd % 2 + 1) * DV], start=True, stop=True)
                mm.then_inc(B["s1_ready"], 1)
                pe.wait_ge(B["s1_done"], z + 1)
            pe.wait_ge(B["lv_done"], 2 * LEVELS)
            pe.wait_ge(B["qb_done"], 2)
            for t in range(TC):
                for h2 in range(2):
                    for hh in range(2):
                        hd = 2 * h2 + hh
                        dst = PSA[:, 4 + 2 * t + h2, hh * DV:(hh + 1) * DV]
                        pe.matmul(dst, ST[:, hd, t, :], zl[:, t, 8 + h2, hh * DV:(hh + 1) * DV], start=True, stop=False)
                        pe.matmul(dst, qB[:, 0, hd, t * P:(t + 1) * P], (S1[0][:, hd, :] if t else S0[:, 0, hd, :]), start=False, stop=False)
                        mm = pe.matmul(dst, qB[:, 1, hd, t * P:(t + 1) * P], (S0[:, 1, hd, :] if t else S1[1][:, hd, :]), start=False, stop=True)
                    mm.then_inc(B["go_ready"], 1)

            for n, blk in enumerate((1, 7)):
                for hd in range(H):
                    for t in range(TC):
                        mm = pe.transpose(PSA[:, 2 * n + hd // 2, (hd % 2) * TOK + t * P:(hd % 2) * TOK + (t + 1) * P],
                                          zl[:, t, blk, hd * DK:(hd + 1) * DK], ident)
                mm.then_inc(B["mt_ready"], 1)
            pe.wait_ge(B["go_done"], 4)
            gate_matrix_rows(1)
            pe.wait_ge(B["mr_rev"], 2)
            for w in range(2):
                for z in range(2):
                    for t in range(TC):
                        c = ((w * 2 + z) * TC + t) * 8
                        mm = pe.transpose(PSA[:, 4, c:c + 8], rows[:, (5 if w == 0 else 7) + z, t * P:(t + 1) * P], ident[0:8, 0:8])
            mm.then_inc(B["gc_ready"], 1)
            pe.wait_ge(B["mt_act"], 1)
            pe.wait_ge(B["mt_dve"], 1)
            pe.wait_ge(B["gc_done"], 1)
            for s in range(9):
                if s < 8:
                    z, hd = s // 4, s % 4
                    if s >= 2:
                        pe.wait_ge(B["w_dve"], s - 1)
                        pe.wait_ge(B["qi_done"], s - 1)
                    src = rows[:, 9:11, ::-1] if z else rows[:, 9:11, :]
                    pe.matmul(PSA[:, s % 2, :], ident[0:8, s:s + 1].broadcast_to([8, P]), src, start=True, stop=True).then_inc(B["bc_ready"], 1)
                    if s >= 2:
                        pe.wait_ge(B["sw_done"], s - 1)
                    for t in range(TC):
                        mm = pe.matmul(PSA[:, 2 + s % 2, t * TOK:(t + 1) * TOK], mkT[:, hd, t * P:(t + 1) * P], mqT[:, hd, :], start=True, stop=True)
                    mm.then_inc(B["ms_ready"], 1)
                if s >= 1:
                    r = s - 1
                    z, hd = r // 4, r % 4
                    pe.wait_ge(B["sw_done"], r + 1)
                    if r >= 2:
                        pe.wait_ge(B["mo_done"], r - 1)
                    for jc in range(TC):
                        dst = PSA[:, 4 + 2 * (r % 2) + jc, :]
                        ts_ = [t for t in range(TC) if (t <= jc if z == 0 else t >= jc)]
                        for part in range(2):
                            for n, t in enumerate(ts_):
                                rhs = zl[:, t, 10 + hd // 2, (hd % 2) * DV:(hd % 2 + 1) * DV] if part == 0 else cA("ones")[:, 0:2]
                                c = slice(0, DV) if part == 0 else slice(DV, DV + 2)
                                pe.matmul(dst[:, c], WW[:, r % 2, t, jc * P:(jc + 1) * P], rhs, start=n == 0, stop=False)
                            mm = pe.matmul(dst[:, c], qI[:, r % 2, jc * P:(jc + 1) * P], CN[:, z, hd, c], start=False, stop=True)
                    mm.then_inc(B["mo_ready"], 1)
            pe.wait_ge(B["mo_done"], 8)
            gate_rows(2 * KD)
            pe.wait_ge(B["gt_done"], 1)
            transposes(4, range(4))
            stream(BY["out2"], u0=32, between=rest_of_transposes(BY["out2"], 4))
            pe.wait_ge(acc_free, BY["up2_0"].blk0)
            gate_rows(5 * KD)
            pe.wait_ge(B["gt_done"], 2)
            transposes(5, range(8))
            for g in range(len(GROUP2)):
                for p in PH:
                    if p.name.startswith(f"up2_{g}"):
                        stream(p, u0=40 if p.name == "up2_0" else None)
                stream(BY[f"dn2_{g}"], a0=4 * GROUPS1 + 8 * g)

        @block.scalar
        def _(act):
            ch = Chain(act, act_step)
            AF = act.activation

            def evacuate(p, i, b):
                end = p.seq0 + (b + 1) * p.per_block + i * p.per_iter
                nb = i * p.blocks + b
                buf = (b % 2) if p.blocks % 2 == 0 else p.blk0 % 2
                if p.mod:
                    mb = p.mod0 + nb
                    act.wait_ge(tile_used, end)
                    if not (isinstance(mb, int) and mb == 0):
                        act.wait_ge(mini_ready, mb)
                    AF(modrow[0:4, :], PSA[0:4, 4 + 2 * (b % 2), :], ACT.Copy).then_inc(row_done, 1)
                if p.evac in ("z1", "zc", "zl"):
                    act.wait_ge(tile_used, end)
                    z = {"z1": z1[:, :, :].rearrange("p t (n c) -> p t n c", c=512), "zc": zc, "zl": zl}[p.evac]
                    AF(z[:, 0, nb, :], acc[:, 2 * buf, :], ACT.Copy)
                    AF(z[:, 1, nb, :], acc[:, 2 * buf + 1, :], ACT.Copy).then_inc(acc_free, 1)
                if p.name in SUMMED:
                    act.wait_ge(acc_free, p.blk0 + nb + 1)
                    for t in range(TC):
                        c = (list(SUMMED).index(p.name) * 4 + nb) * 2 + t
                        if c:
                            act.wait_ge(sq_part, c)
                        AF((junk2 if p.name == "dn1_3" else junk1)[:, :], h[:, t, nb * NBLK:(nb + 1) * NBLK], ACT.Square,
                           accum_out=part[:, t, nb:nb + 1]).then_inc(sq_part, 1)
                if p.evac == "up1":
                    ab = int(p.name[4]) * 4 + nb + 1
                    act.wait_ge(acc_free, p.blk0 + nb + 1)
                    AF(sq[:, :], rl[:, :], ACT.Square).then_inc(act_sq, 1)
                    act.wait_ge(act_sq, ab)
                    AF(ahi[:, :, :].rearrange("p (n f) t -> p n (f t)", f=4)[:, nb, :], sq[:, :], ACT.Copy).then_inc(a_hi, 1)
                if p.evac == "up2":
                    ab = nb + 1 + A0[p.name]
                    w = 2 if p.main == 8 else 1
                    act.wait_ge(cv_done, ab)
                    AF(sl[:, 0:w, :], cv[:, 0:w, :], ACT.Silu).then_inc(sl_done, 1)
                    act.wait_ge(acc_free, p.blk0 + nb + 1)
                    if w == 2:
                        dst = ahi[:, :, :].rearrange("p (n f) t -> p n f t", f=2)[:, nb + p.dest // 2, :, :]
                    else:
                        dst = ahi[:, p.dest:p.dest + 1, :]
                    AF(dst, sv[:, 0:w, :], ACT.Copy).then_inc(a_hi, 1)

            def split(p, i, t):
                n = p.seq0 + t
                w = TW
                if p.k == 11 and (t % p.per_block) == p.per_block - 1:
                    w = NBLK
                act.wait_ge(arrived[n % SLOTS], 16 * (n // SLOTS + 1) + i * (2 * p.per_iter))
                AF(whi[:, n % SLOTS, 0:w], raw[:, n % SLOTS, 0:w], ACT.Copy).then_inc(hi_done, 1)

            def low_rank(x):
                act.wait_ge(B["nar_ready"], x + 1)
                AF(glrT[:, :], PSA[0:32, 4, 0:TOK], ACT.Copy).then_inc(B["glr_done"], 1)

            def gates(x, part):
                if part == 0:
                    act.wait_ge(B["dec_done"], x + 1)
                    ch.link(AF(TM[:, :], LA[:, :], ACT.Abs))
                elif part == 1:
                    ch.link(AF(TM[:, :], TM[:, :], ACT.Exp, scale=-1.0))
                else:
                    AF(TM[:, :], TM[:, :], ACT.Ln, bias=1.0).then_inc(B["abs_done"], 1)

            def stream(p, flush, between={}):
                def body(i):
                    for b in range(p.blocks):
                        for t in range(p.per_block):
                            split(p, i, b * p.per_block + t)
                            if t == p.lead - 1:
                                if b > 0:
                                    evacuate(p, i, b - 1)
                                elif isinstance(i, int) and i == 0:
                                    flush()
                                else:
                                    evacuate(p, i - 1, p.blocks - 1)
                            if isinstance(i, int) and i == 0 and (b, t) in between:
                                between[b, t]()
                            if p.name in NARROW and isinstance(i, int) and i == 0:
                                if (b, t) == (0, 6):
                                    low_rank(NARROW[p.name])
                                if b == 1 and t >= 5:
                                    gates(NARROW[p.name], t - 5)
                            if p.name in NARROW and not isinstance(i, int) and b == 0 and t == 0:
                                act.wait_ge(B["gate_done"], NARROW[p.name] + 1)
                turns(act, p.iters, body)

            def deviation(s):
                act.wait_ge(varr, s + 1)
                AF(stat[:, s, 2:4], stat[:, s, 0:2], ACT.Sqrt).then_inc(stdd, 1)

            def sum_squares(s, src):
                for t in range(TC):
                    if src is xc and t:
                        act.wait_ge(sumsq, s + t)
                    AF(junk[:, :] if src is xc else xn[:, t, :], src[:, t, :], ACT.Square, accum_out=stat[:, s, t:t + 1]).then_inc(sumsq, 1)
                deviation(s)

            def transposes_hi(j, ns=range(8)):
                buf = tpy if j in (2, 4) else tpv
                for n in ns:
                    act.wait_ge(tp_val, 8 * j + n + 1)
                    AF(uhi[:, 2 * n:2 * n + 2, :], buf[:, n % 2, :], ACT.Copy).then_inc(tp_hi, 1)

            def start():
                act.wait_ge(ld["vec"], 16)
                AF(csilu[:, :, :], vec[:, OFF_V["c"][0]:OFF_V["c"][0] + 2 * KD], ACT.Silu).then_inc(silu_done, 1)
                act.wait_ge(ld["x"], 32)
                sum_squares(0, h)

            def mix1():
                for s in range(NH + 3):
                    if s < NG:
                        act.wait_ge(fa_ready, 2 * s + 1)
                        if s >= 2:
                            act.wait_ge(fb_ready, s - 1)
                        AF(AB[:, s % 2, 0, :], PSA[:, 0, :], ACT.Copy).then_inc(fa_act, 1)
                    g = s - 1
                    if 0 <= g < NG:
                        act.wait_ge(fb_ready, g + 1)
                        if g >= 1:
                            act.wait_ge(fc_ready, g)
                        AF(re[:, :, :], PSA[:, 2, :], ACT.Copy).then_inc(fb_done, 1)
                    g = s - 2
                    if 0 <= g < NG:
                        act.wait_ge(fc_ready, g + 1)
                        AF(uhi[:, 2 * g:2 * g + 2, :], PSA[:, 3, :], ACT.Copy).then_inc(fc_hi, 1)
                    if s < NH:
                        act.wait_ge(qk_ready, s + 1)
                        if s >= 2:
                            act.wait_ge(sc_ready, s - 1)
                        AF(qk[:, s % 2, :], PSA[:, 4, :], ACT.Copy).then_inc(qk_done, 1)
                    hd = s - 1
                    if 0 <= hd < NH:
                        act.wait_ge(neg_max, hd + 1)
                        for t in range(TC):
                            AF(lg[:, hd % 2, t, :], lg[:, hd % 2, t, :], ACT.Exp, bias=astat[:, hd, t:t + 1],
                               accum_out=astat[:, hd, 2 + t:3 + t]).then_inc(exp_done, 1)
                    hd = s - 2
                    if 0 <= hd < NH:
                        act.wait_ge(pt_ready, hd + 1)
                        if hd >= 2:
                            act.wait_ge(o_ready, hd - 1)
                        AF(pT[:, hd % 2, :, :], PSA[:, 6, :], ACT.Copy).then_inc(pt_done, 1)
                    hd = s - 3
                    if 0 <= hd < NH:
                        act.wait_ge(o_ready, hd + 1)
                        AF(uhi[:, 8 + hd, :], PSA[:, 7, 0:TOK], ACT.Copy).then_inc(o_hi, 1)

            def norm(j, s):
                deviation(s)
                transposes_hi(j)

            def context():
                deviation(3)
                act.wait_ge(ld["ws"], 16)
                AF(wsh[:, :, :], wsr[:, :, :], ACT.Copy).then_inc(B["ws_split"], 1)

            def context_states():
                act.wait_ge(B["suf_ready"], 1)
                for n in range(4):
                    AF(KE[:, n, :], PSA[:, n, :], ACT.Exp).then_inc(B["suf_exp"], 1)
                act.wait_ge(B["w_arg"], 1)
                AF(rows[:, 5, :], rows[:, 4, :], ACT.Exp, bias=mctx[:, 1:2]).then_inc(B["mr_exp"], 1)
                for n in range(4):
                    act.wait_ge(B["st_ready"], n + 1)
                    AF(S0[:, n // 2, 2 * (n % 2):2 * (n % 2) + 2, :], PSA[:, n, :], ACT.Copy).then_inc(B["st_done"], 1)
                for n in range(8):
                    act.wait_ge(B["cn_ready"], n + 1)
                    AF(CN[:, n // 4, n % 4, :], PSA[:, 4 + n % 2, 0:DV + 2], ACT.Copy).then_inc(B["cn_done"], 1)
                sum_squares(4, h)
                transposes_hi(3)

            def heads2():
                act.wait_ge(B["cum_ready"], 1)
                AF(bT[:, :, :], PSA[:, 6:8, :], ACT.Copy).then_inc(B["cum_done"], 1)
                act.wait_ge(B["gqt_ready"], 1)
                AF(gqT[:, :, :], PSA[:, 0:2, :], ACT.Copy, scale=DK ** -0.5).then_inc(B["gqt_act"], 1)
                for z in range(2):
                    if z:
                        act.wait_ge(B["cum_ready"], 2)
                        act.wait_ge(B["qb_done"], 1)
                        AF(bT[:, :, :], PSA[:, 0:2, :], ACT.Copy).then_inc(B["cum_done"], 1)
                    for n in range(LEVELS):
                        m = z * LEVELS + n
                        act.wait_ge(B["e_sub"], m + 1)
                        ee = EEs[m % 2]
                        ch.link(AF(ee[:, :, :], ee[:, :, :], ACT.Abs))
                        AF(ee[:, :, :], ee[:, :, :], ACT.Exp, scale=-1.0).then_inc(B["e_exp"], 1)
                    act.wait_ge(B["qe_done"], (z + 1) * LEVELS)
                    act.wait_ge(B["ke2_done"], (z + 1) * LEVELS)
                    AF(EE[:, :, :], bT[:, :, :], ACT.Exp).then_inc(B["eb_exp"], 1)
                    act.wait_ge(B["kt_ready"], z + 1)
                    AF(kte[:, :], PSA[:, 4, :], ACT.Exp).then_inc(B["kt_exp"], 1)
                for n in range(4):
                    act.wait_ge(B["go_ready"], n + 1)
                    AF(zl[:, n // 2, 6 * (n % 2), :], PSA[:, 4 + n, :], ACT.Copy).then_inc(B["go_done"], 1)
                act.wait_ge(B["mt_ready"], 1)
                act.wait_ge(B["qb_done"], 2)
                AF(mqT[:, :, :], PSA[:, 0:2, :], ACT.Copy).then_inc(B["mt_act"], 1)
                for t in range(TC):
                    AF(zl[:, t, 2:4, :], zl[:, t, 2:4, :], ACT.Silu).then_inc(B["silu_g"], 1)
                for t in range(TC):
                    AF(zl[:, t, 4:6, :], zl[:, t, 4:6, :], ACT.Sigmoid).then_inc(B["silu_g"], 1)
                act.wait_ge(B["w_arg"], 2)
                AF(rows[:, 7, :], rows[:, 8, :], ACT.Exp, scale=-1.0)
                AF(rows[:, 10, :], rows[:, 9, :], ACT.Exp, bias=mctx[:, 0:1]).then_inc(B["mr_exp"], 1)
                for s in range(8):
                    act.wait_ge(B["w_dve"], s + 1)
                    AF(WW[:, s % 2, :, :], WW[:, s % 2, :, :], ACT.Exp).then_inc(B["w_act"], 1)
                act.wait_ge(B["mo_done"], 8)
                for t in range(TC):
                    for n in range(8):
                        blk = (0, 6, 1, 7)[n // 2]
                        AF(sqj[:, t, n, :], zl[:, t, blk, (n % 2) * DV:(n % 2 + 1) * DV], ACT.Square,
                           accum_out=rst[:, 0, t, n:n + 1]).then_inc(B["ss_done"], 1)
                act.wait_ge(B["rs_var"], 1)
                AF(rst[:, 1, :, :], rst[:, 0, :, :], ACT.Sqrt).then_inc(B["rs_std"], 1)
                transposes_hi(4)

            interlude = {"in1": mix1, "out1": lambda: norm(1, 1), "dn1_3": context,
                         "inC": context_states, "inL": heads2,
                         "out2": lambda: norm(5, 5)}
            def context_squares():
                act.wait_ge(ld["xc"], 32)
                act.wait_ge(a_ready, 4 * GROUPS1)
                sum_squares(2, xc)

            ctx_norm = {(1, 0): context_squares}
            for n in range(4):
                ctx_norm[1, 4 + n] = lambda n=n: transposes_hi(2, (2 * n, 2 * n + 1))
            start()
            flush = lambda: transposes_hi(0)
            for p in PH:
                stream(p, flush, ctx_norm if p.name == "dn1_3" else {})

                def flush(p=p):
                    evacuate(p, p.iters - 1, p.blocks - 1)
                    if p.name in interlude:
                        interlude[p.name]()
            flush()
            deviation(6)

        @block.vector
        def _(dve):
            ch = Chain(dve, dve_step)

            def mod_add(mb):
                dve.wait_ge(mini_ready, mb + 1)
                bm = v_("b_mod").rearrange("p (n c) -> p n c", c=4)[:, mb, :]
                TT(modT[:, :, :].rearrange("p (n c) w -> p n c w", c=4)[:, mb, :, :],
                   PSA[:, 5, 0:8].rearrange("p (c w) -> p c w", w=2), bm.unsqueeze(2).broadcast_to([P, 4, 2]), ALU.add).then_inc(mini_done, 1)

            TT, TS, STT, CP = dve.tensor_tensor, dve.tensor_scalar, dve.scalar_tensor_tensor, dve.tensor_copy

            def evacuate(p, i, b):
                end = p.seq0 + (b + 1) * p.per_block + i * p.per_iter
                nb = i * p.blocks + b
                ch = Chain(dve, evac_step, E0[p.name] + STEPS.get(p.evac, 0) * nb)
                buf = (b % 2) if p.blocks % 2 == 0 else p.blk0 % 2
                if p.evac == "res":
                    dve.wait_ge(tile_used, end)
                    hb = h[:, :, :].rearrange("p t (n c) -> p t n c", c=512)[:, :, nb, :]
                    TT(hb, acc[:, 2 * buf:2 * buf + 2, :], hb, ALU.add).then_inc(acc_free, 1)
                if p.evac == "gres":
                    dve.wait_ge(tile_used, end)
                    hb = h[:, :, :].rearrange("p t (n c) -> p t n c", c=512)[:, :, nb, :]
                    gb = gtb[:, :].rearrange("p (n c) -> p n c", c=512)[:, nb, :]
                    for t in range(TC):
                        ins = TT(gtmp[:, t, :], acc[:, 2 * buf + t, :], gb, ALU.mult)
                    ch.link(ins)
                    TT(hb, gtmp[:, :, :], hb, ALU.add).then_inc(acc_free, 1)
                if p.evac == "up1":
                    ab = int(p.name[4]) * 4 + nb + 1
                    dve.wait_ge(tile_used, end)
                    TS(rl[:, :], acc[:, 2 * buf:2 * buf + 2, :], 0.0, None, ALU.max).then_inc(acc_free, 1)
                    dve.wait_ge(a_hi, ab)
                    f4 = "p (n f) t -> p n (f t)"
                    TT(alo[:, :, :].rearrange(f4, f=4)[:, nb, :], sq[:, :], ahi[:, :, :].rearrange(f4, f=4)[:, nb, :],
                       ALU.subtract).then_inc(a_ready, 1)
                if p.evac == "up2":
                    ab = nb + 1 + A0[p.name]
                    w = 2 if p.main == 8 else 1
                    dve.wait_ge(tile_used, end)
                    ck = int(p.name[4]) * 16 + p.dest + i * (2 * p.blocks) + 2 * b
                    cwv = v_("conv_w").rearrange("p (n k) -> p n k", k=9)
                    cbv = v_("conv_b").rearrange("p (n k) -> p n k", k=1)
                    gate = [acc[:, 2 * buf + n, 0:TOK].rearrange("p (r c) -> p r c", c=64) for n in range(w)]
                    cvv = [cv[:, n, :].rearrange("p (r c) -> p r c", c=64) for n in range(w)]
                    for n in range(w):
                        last = TS(cvv[n], gate[n], cwv[:, ck + n, 4:5], cbv[:, ck + n, :], ALU.mult, ALU.add)
                    ch.link(last)
                    for tap in (0, 1, 2, 3, 5, 6, 7, 8):
                        dr, dc = tap // 3 - 1, tap % 3 - 1
                        ro = slice(max(0, -dr), 4 - max(0, dr))
                        ri = slice(max(0, dr), 4 + min(0, dr))
                        co = slice(max(0, -dc), 64 - max(0, dc))
                        ci = slice(max(0, dc), 64 + min(0, dc))
                        for n in range(w):
                            last = STT(cvv[n][:, ro, co], gate[n][:, ri, ci], cwv[:, ck + n, tap:tap + 1], cvv[n][:, ro, co], ALU.mult, ALU.add)
                        if tap < 8:
                            ch.link(last)
                        else:
                            last.then_inc(cv_done, 1)
                    dve.wait_ge(sl_done, ab)
                    TT(sv[:, 0:w, :], acc[:, 2 * buf:2 * buf + w, TOK:2 * TOK], sl[:, 0:w, :], ALU.mult).then_inc(acc_free, 1)
                    dve.wait_ge(a_hi, 4 * GROUPS1 + ab)
                    if w == 2:
                        f2 = "p (n f) t -> p n f t"
                        dh = ahi[:, :, :].rearrange(f2, f=2)[:, nb + p.dest // 2, :, :]
                        dl = alo[:, :, :].rearrange(f2, f=2)[:, nb + p.dest // 2, :, :]
                    else:
                        dh, dl = ahi[:, p.dest:p.dest + 1, :], alo[:, p.dest:p.dest + 1, :]
                    TT(dl, sv[:, 0:w, :], dh, ALU.subtract).then_inc(a_ready, 1)

            def split(p, i, t):
                n = p.seq0 + t
                w = TW
                if p.k == 11 and (t % p.per_block) == p.per_block - 1:
                    w = NBLK
                dve.wait_ge(hi_done, n + 1 + i * p.per_iter)
                TT(wlo[:, n % SLOTS, 0:w], raw[:, n % SLOTS, 0:w], whi[:, n % SLOTS, 0:w], ALU.subtract).then_inc(lo_done, 1)

            LAf = LA[:, 2048:2064].rearrange("p (t z h) -> p t z h", t=TC, z=2)

            def gates(x):
                dve.wait_ge(B["glr_ready"], x + 1)
                CP(sm[:, :, :], PSA[:, 5, 0:64]).then_inc(B["nar_done"], 1)
                dve.wait_ge(B["nar_done"], x + 1)
                ch.link(dve.memset(gm[:, :, :, :, :], 0.0))
                for z in range(2):
                    c = 16 + 8 * z
                    TT(gm[:, :, z, 0, 4 * z:4 * z + 4], sm[:, :, c:c + 4], bgate[:, 8 * z:8 * z + 4].unsqueeze(1).broadcast_to([P, TC, 4]), ALU.add)
                    TT(LAf[:, :, z, :], sm[:, :, c + 4:c + 8], bgate[:, 8 * z + 4:8 * z + 8].unsqueeze(1).broadcast_to([P, TC, 4]), ALU.add)

            def gates_mid(x):
                dve.wait_ge(ld["bl"], 16)
                dve.wait_ge(B["dec_ready"], x + 1)
                for t in range(TC):
                    ins = TT(LA[:, t * 1024:(t + 1) * 1024], PSA[:, 4 + 2 * t:6 + 2 * t, :], blr[:, :, :], ALU.add)
                ins.then_inc(B["dec_done"], 1)

            def gates_end(x):
                dve.wait_ge(B["abs_done"], x + 1)
                STT(LA[:, :], LA[:, :], 0.0, TM[:, :], ALU.min, ALU.subtract).then_inc(B["gate_done"], 1)
                dve.wait_ge(B["gate_done"], x + 1)
                for z in range(2):
                    ins = CP(gm[:, :, z, 1, 4 * z:4 * z + 4], LAf[:, :, z, :])
                ins.then_inc(B["gm_done"], 1)

            def stream(p, flush, before, between={}):
                def body(i):
                    for b in range(p.blocks):
                        for t in range(p.per_block):
                            split(p, i, b * p.per_block + t)
                            if t == 7:
                                new = b == 0 and isinstance(i, int) and i == 0
                                if p.mod and not new:
                                    mod_add(p.mod0 + b - 1 + i * p.blocks)
                                if new and before is not None:
                                    mod_add(before.mod0 + before.iters * before.blocks - 1)
                            if t == p.lead - 1:
                                if b > 0:
                                    evacuate(p, i, b - 1)
                                elif isinstance(i, int) and i == 0:
                                    flush()
                                else:
                                    evacuate(p, i - 1, p.blocks - 1)
                            if isinstance(i, int) and i == 0 and (b, t) in between:
                                between[b, t]()
                            if p.name in NARROW and isinstance(i, int) and i == 0:
                                if b == 1 and t == 0:
                                    gates(NARROW[p.name])
                                if b == 1 and t == 4:
                                    gates_mid(NARROW[p.name])
                turns(dve, p.iters, body, (lambda: gates_end(NARROW[p.name])) if p.name in NARROW else masks_as_bytes if p.name == "in1" else None)

            def masks_as_bytes():
                dve.wait_ge(ld["lev"], 16)
                ch.link(CP(levels[:, :], lev_in[:, :]))

            def variance(s, width=D):
                if s in SUMMED.values():
                    dve.wait_ge(sq_part, 8 * (list(SUMMED.values()).index(s) + 1))
                    ch.link(dve.tensor_reduce(stat[:, s, 0:2], part[:, :, :], axis=AX.X, op=ALU.add))
                else:
                    dve.wait_ge(sumsq, s + 2)
                TS(stat[:, s, 0:2], stat[:, s, 0:2], 1.0 / width, eps, ALU.mult, ALU.add).then_inc(varr, 1)
                dve.wait_ge(stdd, s + 1)
                ch.link(dve.reciprocal(stat[:, s, 2:4], stat[:, s, 2:4]))

            def transposes_lo(j, A, Bc, ns=range(8)):
                buf = tpy if j in (2, 4) else tpv
                banks = (4, 5, 6, 7) if j == 2 else (2, 3, 5, 7)

                def low(n):
                    dve.wait_ge(tp_hi, 8 * j + n + 1)
                    TT(ulo[:, 2 * n:2 * n + 2, :], buf[:, n % 2, :].rearrange("p (k t) -> p k t", k=2), uhi[:, 2 * n:2 * n + 2, :],
                       ALU.subtract).then_inc(u_ready, 1)
                for n in ns:
                    dve.wait_ge(tp_ready, 8 * j + n + 1)
                    if n >= 2:
                        dve.wait_ge(u_ready, 8 * j + n - 1)
                    if A is None:
                        CP(buf[:, n % 2, :], PSA[:, banks[n % 4], :]).then_inc(tp_val, 1)
                    else:
                        for kk in range(2):
                            k = 2 * n + kk
                            ins = TS(buf[:, n % 2, kk * TOK:(kk + 1) * TOK], PSA[:, banks[n % 4], kk * TOK:(kk + 1) * TOK],
                                     A[:, k:k + 1], (Bc[:, k:k + 1] if Bc is not None else 0.0), ALU.mult, ALU.add)
                        ins.then_inc(tp_val, 1)
                    if n > ns[0]:
                        low(n - 1)
                low(ns[-1])

            def normalise(s, src, dst=xn):
                for t in range(TC):
                    TS(dst[:, t, :], src[:, t, :], stat[:, s, 2 + t:3 + t], None, ALU.mult).then_inc(xn_done, 1)

            def norm(j, s, src, A, Bc):
                variance(s)
                normalise(s, src)
                transposes_lo(j, A, Bc)

            def modulated(n, scale, who, g):
                m = modT[:, scale * KD:(scale + 1) * KD, who]
                ch.link(STT(colA[:, n, :], m, 1.0, v_(g), ALU.add, ALU.mult))
                return colA[:, n, :]

            def shift(n, who):
                return modT[:, n * KD:(n + 1) * KD, who]

            def start():
                ch.link(dve.memset(cst[:, :, :].bitcast(F32), 0.0))
                dve.wait_ge(silu_done, 1)
                for w in range(2):
                    ch.link(CP(cst[:, :, 2 * w], csilu[:, w, :]))
                    ins = TT(cst[:, :, 2 * w + 1], csilu[:, w, :], cst[:, :, 2 * w], ALU.subtract)
                    if w == 0:
                        ch.link(ins)
                ins.then_inc(c_done, 1)
                variance(0)
                normalise(0, h)

            def mix1():
                dve.wait_ge(ld["cb"], 32)
                for s in range(NH + 3):
                    if s == 0:
                        ch.link(STT(bias[:, :], cB("dist"), -(2.0 ** (-8.0 / NH)), cB("logcount"), ALU.mult, ALU.add))
                    if s < NG:
                        dve.wait_ge(fa_ready, 2 * s + 2)
                        if s >= 2:
                            dve.wait_ge(fb_ready, s - 1)
                        CP(AB[:, s % 2, 1, :], PSA[:, 1, :]).then_inc(fa_dve, 1)
                    g = s - 2
                    if 0 <= g < NG:
                        dve.wait_ge(fc_hi, g + 1)
                        TT(ulo[:, 2 * g:2 * g + 2, :], PSA[:, 3, :], uhi[:, 2 * g:2 * g + 2, :], ALU.subtract).then_inc(fc_lo, 1)
                    hd = s - 1
                    if 0 <= hd < NH:
                        dve.wait_ge(sc_ready, hd + 1)
                        if hd >= 2:
                            dve.wait_ge(pt_ready, hd - 1)
                        L = lg[:, hd % 2, :, :]
                        ch.link(STT(L, PSA[:, 5, :], DH ** -0.5, bias[:, :], ALU.mult, ALU.add))
                        dve.tensor_reduce(astat[:, hd, 0:2], L, axis=AX.X, op=ALU.max, negate=True).then_inc(neg_max, 1)
                        if hd + 1 < NH:
                            ch.link(STT(bias[:, :], cB("dist"), -(2.0 ** (-8.0 * (hd + 2) / NH)), cB("logcount"), ALU.mult, ALU.add))
                        dve.wait_ge(exp_done, 2 * hd + 2)
                        ch.link(dve.reciprocal(astat[:, hd, 4:6], astat[:, hd, 2:4]))
                        for t in range(TC):
                            ins = TS(lg[:, hd % 2, t, :], lg[:, hd % 2, t, :], astat[:, hd, 4 + t:5 + t], None, ALU.mult)
                        ins.then_inc(prob_done, 1)
                    hd = s - 3
                    if 0 <= hd < NH:
                        dve.wait_ge(o_hi, hd + 1)
                        TT(ulo[:, 8 + hd, :], PSA[:, 7, 0:TOK], uhi[:, 8 + hd, :], ALU.subtract).then_inc(o_lo, 1)

            def final(s, after):
                variance(s)
                dve.wait_ge(ld["gf"], 16 if s == 3 else 32)
                g = gfin1 if s == 3 else gfin
                for t in range(TC):
                    STT(h[:, t, :], h[:, t, :], stat[:, s, 2 + t:3 + t], g[:, :], ALU.mult, ALU.mult).then_inc(after, 1)

            def context():
                final(3, h_final)
                dve.wait_ge(B["ws_split"], 1)
                TT(wsl[:, :, :], wsr[:, :, :], wsh[:, :, :], ALU.subtract).then_inc(B["ws_low"], 1)

            def gate_rows_sum(x):
                dve.wait_ge(B["row_ready"], x + 1)
                CP(rows[:, 0:2, :], PSA[0:8, 6, :])
                ch.link(dve.memset(rows[:, 3, :], 0.0))
                ch.link(dve.tensor_tensor_scan(rows[:, 2, :], rows[:, 1, :], rows[:, 3, :], 0.0, ALU.add, ALU.add))

            def context_states():
                for n in range(4):
                    z, t = n // 2, n % 2
                    dve.wait_ge(B["suf_exp"], n + 1)
                    TT(KE[:, n, :], KE[:, n, :], zc[:, t, 0, :], ALU.mult).then_inc(B["ke_done"], 1)
                gate_rows_sum(0)
                end = rows[:, 2, TOK - 1:TOK]
                ch.link(TS(rows[:, 4, :], rows[:, 2, :], -1.0, end, ALU.mult, ALU.add))
                ch.link(TT(rows[:, 4, :], rows[:, 4, :], rows[:, 0, :], ALU.add))
                ch.link(dve.tensor_reduce(mctx[:, 0:1], rows[:, 4, :], axis=AX.X, op=ALU.max))
                ch.link(TT(mctx[:, 0:1], mctx[:, 0:1], end, ALU.max))
                TS(mctx[:, 1:2], mctx[:, 0:1], -1.0, None, ALU.mult).then_inc(B["w_arg"], 1)
                dve.wait_ge(B["mr_exp"], 1)
                CP(rows[:, 6, :], rows[:, 5, ::-1]).then_inc(B["mr_rev"], 1)
                dve.wait_ge(B["wc_ready"], 1)
                ch.link(TS(wcol[:, :, :, :], PSA[:, 7, 0:32].rearrange("p (z t e) -> p z t e", z=2, t=TC), DK ** -0.5, None, ALU.mult))
                for n in range(4):
                    z, t = n // 2, n % 2
                    TT(WK[:, n, :].rearrange("p (e k) -> p e k", e=H), zc[:, t, 1, :].rearrange("p (e k) -> p e k", e=H),
                       wcol[:, z, t, 4 * z:4 * z + 4].unsqueeze(2).broadcast_to([P, H, DK]), ALU.mult).then_inc(B["wk_done"], 1)
                norm(3, 4, h, modulated(3, 1, 0, "g_n1"), shift(0, 0))

            def heads2():
                def take(m):
                    z, n = m // LEVELS, m % LEVELS
                    b0 = 2 if m % 2 else 6
                    dve.wait_ge(B["lv_ready"], m + 1)
                    if m:
                        dve.wait_ge(B["lv_done"], m)
                    mask = levels[:, m * P:(m + 1) * P].unsqueeze(1).broadcast_to([P, 8, P])
                    dve.copy_predicated(STf, mask, PSA[:, b0:b0 + 2, :].rearrange("p b (c j) -> p (b c) j", j=P)).then_inc(B["lv_done"], 1)

                def decay_from_mid(z, n):
                    m = z * LEVELS + n
                    L = 2 ** n
                    if m >= 2:
                        dve.wait_ge(B["ke2_done"], m - 1)
                        dve.wait_ge(B["qe_done"], m - 1)
                    if z and n == 1:
                        dve.wait_ge(B["qb_done"], 1)
                    bv = bT[:, :, :].rearrange("p e (b l) -> p (e b) l", l=2 * L)
                    mid = L if z else L - 1
                    TT(EEs[m % 2][:, :, :].rearrange("p e (b l) -> p (e b) l", l=2 * L), bv,
                       bv[:, :, mid:mid + 1].broadcast_to([P, H * TOK // (2 * L), 2 * L]), ALU.subtract).then_inc(B["e_sub"], 1)

                dve.wait_ge(B["cum_done"], 1)
                decay_from_mid(0, 0)
                dve.wait_ge(B["gqt_ready"], 2)
                CP(gkT[:, :, :], PSA[:, 2:4, :]).then_inc(B["gqt_dve"], 1)
                dve.wait_ge(B["dg_ready"], 1)
                two = cA("two_ident").unsqueeze(1).broadcast_to([P, 8, P])
                STf = ST[:, :, :, :].rearrange("p e t j -> p (e t) j")
                TT(STf, PSA[:, 4:6, :].rearrange("p b (c j) -> p (b c) j", j=P), two, ALU.mult).then_inc(B["dg_done"], 1)
                dve.wait_ge(B["dg_done"], 1)

                for z in range(2):
                    if z:
                        dve.wait_ge(B["cum_done"], 2)
                        dve.wait_ge(B["eb_exp"], 1)
                        decay_from_mid(1, 0)
                    for n in range(LEVELS):
                        m = z * LEVELS + n
                        if n + 1 < LEVELS:
                            decay_from_mid(z, n + 1)
                        if m:
                            dve.wait_ge(B["lv_ready"], m)
                        dve.wait_ge(B["e_exp"], m + 1)
                        TT(qE[:, :, :], gqT[:, :, :], EEs[m % 2][:, :, :], ALU.mult).then_inc(B["qe_done"], 1)
                        if m:
                            take(m - 1)
                    if z:
                        take(2 * LEVELS - 1)
                    dve.wait_ge(B["eb_exp"], z + 1)
                    TT(qB[:, z, :, :], gqT[:, :, :], EE[:, :, :], ALU.mult)
                    col = P if z else P - 1
                    CP(ebend[:, z, :], EE[:, :, col]).then_inc(B["qb_done"], 1)
                    dve.wait_ge(B["kt_exp"], z + 1)
                    TT(kte[:, :], kte[:, :], zl[:, z, 6, :], ALU.mult).then_inc(B["kt_done"], 1)
                    dve.wait_ge(B["s1_ready"], z + 1)
                    dve.wait_ge(B["qb_done"], z + 1)
                    for hd in range(H):
                        ins = STT(S1[z][:, hd, :], S0[:, z, hd, :], ebend[:, z, hd:hd + 1],
                                  PSA[:, hd // 2, (hd % 2) * DV:(hd % 2 + 1) * DV], ALU.mult, ALU.add)
                    ins.then_inc(B["s1_done"], 1)
                dve.wait_ge(B["mt_ready"], 2)
                TS(mkT[:, :, :], PSA[:, 2:4, :], DK ** -0.5, None, ALU.mult).then_inc(B["mt_dve"], 1)
                dve.wait_ge(B["go_done"], 4)
                gate_rows_sum(1)
                ch.link(TT(rows[:, 5, :], rows[:, 0, :], rows[:, 2, :], ALU.subtract))
                ch.link(dve.tensor_tensor_scan(rows[:, 4, :], rows[:, 5, :], rows[:, 5, :], mctx[:, 0:1], ALU.max, ALU.max))
                TS(rows[:, 9, :], rows[:, 4, :], -1.0, None, ALU.mult)
                TT(rows[:, 8, :], rows[:, 4, :], rows[:, 2, :], ALU.add).then_inc(B["w_arg"], 1)
                CP(rows[:, 6, :], rows[:, 5, ::-1])
                dve.wait_ge(B["mr_exp"], 2)
                CP(rows[:, 8, :], rows[:, 7, ::-1]).then_inc(B["mr_rev"], 1)
                dve.wait_ge(B["gc_ready"], 1)
                CP(gcol[:, :, :, :, :], PSA[:, 4, 0:64]).then_inc(B["gc_done"], 1)
                dve.wait_ge(B["gc_done"], 1)
                dve.wait_ge(ld["mm"], 16)

                def output(r):
                    z, hd = r // 4, r % 4
                    dve.wait_ge(B["mo_ready"], r + 1)
                    for jc in range(TC):
                        b_ = PSA[:, 4 + 2 * (r % 2) + jc, :]
                        ch.link(TS(hden[:, r % 2, jc, 2:3], b_[:, DV:DV + 1], -1.0, None, ALU.mult))
                        ch.link(TS(hden[:, r % 2, jc, 0:1], b_[:, DV:DV + 1], hden[:, r % 2, jc, 2:3], gcol[:, 1, z, jc, r:r + 1],
                                   ALU.max, ALU.max))
                    ch.link(dve.reciprocal(hden[:, r % 2, :, 1], hden[:, r % 2, :, 0]))
                    for jc in range(TC):
                        b_ = PSA[:, 4 + 2 * (r % 2) + jc, 0:DV]
                        dst = zl[:, jc, (1 if hd < 2 else 7), (hd % 2) * DV:(hd % 2 + 1) * DV]
                        if z == 0:
                            ins = TS(dst, b_, hden[:, r % 2, jc, 1:2], None, ALU.mult)
                        else:
                            ins = STT(dst, b_, hden[:, r % 2, jc, 1:2], dst, ALU.mult, ALU.add)
                    ins.then_inc(B["mo_done"], 1)

                for s in range(9):
                    if s < 8:
                        z, hd = s // 4, s % 4
                        dve.wait_ge(B["bc_ready"], s + 1)
                        if s >= 2:
                            dve.wait_ge(B["mo_ready"], s - 1)
                        for t in range(TC):
                            ins = STT(WW[:, s % 2, t, :], PSA[:, s % 2, 0:TOK], gcol[:, 0, z, t, s:s + 1], minmask[:, z, t, :], ALU.add, ALU.min)
                        ins.then_inc(B["w_dve"], 1)
                        if s == 0:
                            dve.wait_ge(B["mt_act"], 1)
                        TT(qI[:, s % 2, :], mqT[:, hd, :], PSA[:, s % 2, TOK:2 * TOK], ALU.mult).then_inc(B["qi_done"], 1)
                        dve.wait_ge(B["w_act"], s + 1)
                        dve.wait_ge(B["ms_ready"], s + 1)
                        TT(WW[:, s % 2, :, :], WW[:, s % 2, :, :], PSA[:, 2 + s % 2, :], ALU.mult).then_inc(B["sw_done"], 1)
                    if s >= 1:
                        if s - 1 == 4:
                            dve.wait_ge(B["mo_done"], 4)
                        output(s - 1)
                gate_banks(0)
                dve.wait_ge(B["ss_done"], 2 * 8)
                TS(rst[:, 0, :, :], rst[:, 0, :, :], 1.0 / DV, eps, ALU.mult, ALU.add).then_inc(B["rs_var"], 1)
                dve.wait_ge(B["rs_std"], 1)
                ch.link(dve.reciprocal(rst[:, 2, :, :], rst[:, 1, :, :]))
                dve.wait_ge(ld["gn"], 16)
                dve.wait_ge(B["silu_g"], 4)
                for t in range(TC):
                    for n in range(8):
                        o_ = zl[:, t, (0, 6, 1, 7)[n // 2], (n % 2) * DV:(n % 2 + 1) * DV]
                        ins = STT(o_, o_, rst[:, 2, t, n:n + 1], gnb[:, n // 4, :], ALU.mult, ALU.mult)
                    ch.link(ins)
                    for n in range(4):
                        g_ = zl[:, t, 2 + n, :]
                        ins = TT(g_, g_, zl[:, t, (0, 6, 1, 7)[n], :], ALU.mult)
                        if n % 2:
                            ins.then_inc(B["y_done"], 1)
                transposes_lo(4, None, None)

            def gate_banks(x):
                for n in range(4):
                    dve.wait_ge(B["gt_ready"], 4 * x + n + 1)
                    ins = CP(gtb[:, n * 512:(n + 1) * 512], PSA[:, n, :])
                ins.then_inc(B["gt_done"], 1)
                dve.wait_ge(B["gt_done"], x + 1)

            def out2():
                gate_banks(1)
                norm(5, 5, h, modulated(5, 4, 0, "g_n2"), shift(3, 0))

            interlude = {"in1": mix1, "out1": lambda: norm(1, 1, h, v_("g_mlp"), None), "dn1_3": context,
                         "inC": context_states, "inL": heads2, "out2": out2}
            ctx_norm = {(1, 0): lambda: variance(2), (1, 1): lambda: normalise(2, xc, xc), (1, 3): lambda: modulated(2, 1, 1, "g_n1")}
            for n in range(4):
                ctx_norm[1, 4 + n] = lambda n=n: transposes_lo(2, colA[:, 2, :], shift(0, 1), (2 * n, 2 * n + 1))
            start()
            flush = lambda: transposes_lo(0, v_("g_mix"), None)
            before = None
            for p in PH:
                stream(p, flush, before if before is not None and before.mod and before.name != "in1" else None,
                       ctx_norm if p.name == "dn1_3" else {})
                before = p

                def flush(p=p):
                    evacuate(p, p.iters - 1, p.blocks - 1)
                    if p.name == "in1":
                        mod_add(7)
                    if p.name in interlude:
                        interlude[p.name]()
            flush()
            final(6, B["fin_done"])

        @block.gpsimd
        def _(pool):
            for m in range(2 * LEVELS):
                if m == 0:
                    pool.wait_ge(B["gqt_dve"], 1)
                if m >= 2:
                    pool.wait_ge(B["lv_ready"], m - 1)
                pool.wait_ge(B["e_exp"], m + 1)
                dst = kE[:, :, :] if m % 2 == 0 else zl[:, :, 0, :].rearrange("p a (b t) -> p a b t", b=2)
                by_two = "p (a b) t -> p a b t"
                if m % 2:
                    pool.tensor_tensor(dst, gkT[:, :, :].rearrange(by_two, a=2), EE2[:, :, :].rearrange(by_two, a=2), ALU.mult).then_inc(B["ke2_done"], 1)
                else:
                    pool.tensor_tensor(dst, gkT[:, :, :], EE[:, :, :], ALU.mult).then_inc(B["ke2_done"], 1)


def constants():
    s = np.arange(P)
    t = np.arange(TOK)
    a = {"ident": np.eye(P), "flip": np.eye(P)[::-1], "suf": (s[:, None] > s[None, :]) / 16.0, "pre": (s[:, None] < s[None, :]) / 16.0,
         "inc_f": (s[:, None] <= s[None, :]) / 16.0, "inc_b": (s[:, None] >= s[None, :]) / 16.0, "one16": np.ones((P, P)) / 16.0,
         "ones": np.ones((P, P)), "two_ident": 2.0 * np.eye(P)}
    sel4 = np.zeros((P, 2))
    sel4[0:2, 0] = 1.0
    sel4[2:4, 1] = 1.0
    a["sel4"] = sel4
    const_a = np.concatenate([a[n] for n, _ in CONST_A], axis=1).astype(np.float32)

    ang = 2.0 * np.pi * ((t[:, None] * t[None, :]) % TOK) / TOK
    cos, sin = np.cos(ang) / 16.0, np.sin(ang) / 16.0
    chunks = lambda m: m.reshape(TC, P, -1).transpose(1, 0, 2).reshape(P, -1)
    d = np.abs(t[:, None] - t[None, :])
    count = (d <= 64).astype(int) + (d % 4 == 0) + (d % 16 == 0)
    logcount = np.where(count > 0, np.log(np.maximum(count, 1)), NEG)
    b = {"dft_pos": chunks(np.concatenate([cos, sin], axis=1)), "dft_cos": chunks(cos), "dft_nsin": chunks(-sin),
         "dist": chunks(d), "logcount": chunks(logcount)}
    const_b = np.concatenate([b[n] for n, _ in CONST_B], axis=1).astype(np.float32)

    i, j = s[:, None], s[None, :]
    lv = []
    for z in range(2):
        for n in range(LEVELS):
            L = 2 ** n
            same = (i // (2 * L)) == (j // (2 * L))
            first_i, first_j = (i % (2 * L)) < L, (j % (2 * L)) < L
            lv.append(same & first_i & ~first_j if z == 0 else same & ~first_i & first_j)
    levels = np.concatenate(lv, axis=1).astype(np.float32)

    key = s[:, None, None, None] + P * np.arange(TC)[None, None, :, None]
    qry = t[None, None, None, :]
    z = np.arange(2)[None, :, None, None]
    min_mask = np.where(np.where(z == 0, key <= qry, key >= qry), 0.0, NEG).astype(np.float32)
    return {"const_a": const_a, "const_b": const_b, "levels": levels, "min_mask": min_mask}


def token_tiles(w):
    k, n = w.shape
    return np.ascontiguousarray(w.reshape(k // 256, 2, P, n // NBLK, NBLK).transpose(3, 0, 2, 1, 4)).reshape(-1, P, TW)


def feature_tiles(w):
    k, n = w.shape
    return np.ascontiguousarray(w.reshape(2, 8, P, n // P, P).transpose(3, 0, 2, 1, 4)).reshape(-1, P, TW)


def columns(v):
    return np.asarray(v).reshape(-1, P).T


def layout(x, norm_mix_g, w_in, w_fourier, w_out, norm_mlp_g, w_up, w_down, norm_final_g, c_2, ctx_2, c_ctx_2, w_mod_2, b_mod_2,
           g_norm1_2, g_norm2_2, w_in_2, gla_w_lr_2, gla_b_lr_2, mlstm_b_gate_2, gla_g_norm_2, mlstm_g_norm_2, w_out_2, w_up_2,
           conv_w_2, conv_b_2, w_down_2, g_final_2):
    t = dict(constants())
    t["x"], t["ctx"] = np.asarray(x)[0], np.asarray(ctx_2)[0]
    t["w_in"] = token_tiles(np.asarray(w_in)[0])
    t["w_out"] = token_tiles(np.asarray(w_out)[0])
    t["w_up"] = feature_tiles(np.asarray(w_up)[0])
    t["w_down"] = np.concatenate([token_tiles(np.asarray(w_down)[0, q * 2048:(q + 1) * 2048]) for q in range(GROUPS1)])
    t["w_fourier"] = np.asarray(w_fourier)[0].reshape(NG, 2, P, 256).transpose(2, 0, 1, 3)
    t["w_mod"] = token_tiles(np.asarray(w_mod_2)[0])
    w = np.asarray(w_in_2)[0]
    at, part = 0, {}
    for name, n in (("gq", 512), ("gk", 512), ("gv", 1024), ("gg", 1024), ("lr", 16), ("mq", 512), ("mk", 512), ("mv", 1024),
                    ("mo", 1024), ("mg", 16)):
        part[name] = w[:, at:at + n]
        at += n
    t["w_in2"] = token_tiles(np.concatenate([part[n] for n in ("gq", "mq", "gg", "mo", "gk", "mk", "gv", "mv")], axis=1))
    t["w_in2_narrow"] = np.concatenate([part["lr"], part["mg"]], axis=1).reshape(KD, P, 32).transpose(1, 0, 2)
    t["w_lr"] = np.asarray(gla_w_lr_2)[0].transpose(1, 0, 2)
    t["b_lr"] = np.asarray(gla_b_lr_2)[0]
    t["b_gate"] = np.asarray(mlstm_b_gate_2)[0].reshape(16)
    t["g_heads"] = np.stack([np.asarray(gla_g_norm_2)[0], np.asarray(mlstm_g_norm_2)[0]])
    t["w_out2"] = token_tiles(np.asarray(w_out_2)[0])
    w = np.asarray(w_up_2)[0].reshape(D, 2, F2, P).transpose(0, 2, 1, 3).reshape(D, 2 * DFF2)
    t["w_up2"] = feature_tiles(w)
    w = np.asarray(w_down_2)[0]
    t["w_down2"] = np.concatenate([token_tiles(w[g * 2048:(g + 1) * 2048]) for g in range(2)])
    t["w_down2b"] = w[4096:].reshape(GROUP2[2], P, 4, NBLK).transpose(2, 1, 0, 3).reshape(4, P, GROUP2[2] * NBLK)
    t["g_final1"], t["g_final2"] = np.asarray(norm_final_g), np.asarray(g_final_2)
    conv = np.asarray(conv_w_2)[0].reshape(9, F2, P).transpose(2, 1, 0).reshape(P, F2 * 9)
    vec = {"g_mix": columns(norm_mix_g), "g_mlp": columns(norm_mlp_g), "g_n1": columns(g_norm1_2), "g_n2": columns(g_norm2_2),
           "c": columns(c_2), "cc": columns(c_ctx_2), "b_mod": columns(b_mod_2), "conv_w": conv, "conv_b": columns(conv_b_2)}
    t["vec"] = np.concatenate([vec[n] for n, _ in VEC], axis=1)
    return {n: np.ascontiguousarray(a) for n, a in t.items()}


def build(nc, arrays):
    t_in = {n: nc.dram_tensor("in_" + n, a.shape, mybir.dt.from_np(a.dtype), kind="ExternalInput").ap() for n, a in arrays.items()}
    out = nc.dram_tensor("out_0", (TOK, D), F32, kind="ExternalOutput").ap()
    program(nc, t_in, out)


def kernel(**inputs):
    import concourse.bacc as bacc
    from concourse.bass_utils import run_bass_kernel_spmd

    arrays = layout(**inputs)
    nc = bacc.Bacc("TRN2", target_bir_lowering=False, num_devices=1)
    build(nc, arrays)
    r = run_bass_kernel_spmd(nc, [{"in_" + n: a for n, a in arrays.items()}], core_ids=[0])
    return np.asarray(r.results[0]["out_0"]).reshape(1, TOK, D)
```
